# Optimizing a Trainium2 kernel written in Bass

```python
import math
import jax, jax.numpy as jnp
from jax import lax
import numpy as np

D_MODEL = 1024
BATCH = 1
SEQ = 256
DEPTH = 2

N_META = 16
N_A_LAYERS = DEPTH // 2
N_B_LAYERS = DEPTH - N_A_LAYERS
ALPHA = (2.0 * DEPTH) ** 0.25
BETA = (8.0 * DEPTH) ** -0.25
LN_EPS = 1e-5
SSM_EXPAND = 2
D_INNER = SSM_EXPAND * D_MODEL
SSM_HEAD_DIM = 64
SSM_HEADS = D_INNER // SSM_HEAD_DIM
SSM_GROUPS = 4
SSM_HPG = SSM_HEADS // SSM_GROUPS
D_STATE = 128
CONV_WIDTH = 4
SSD_CHUNK = 128
CONV_DIM = D_INNER + 2 * SSM_GROUPS * D_STATE
IN_DIM = D_INNER + CONV_DIM + SSM_HEADS
SB_HEADS = 16
SB_HEAD_DIM = 64
SB_WIDTH = SB_HEADS * SB_HEAD_DIM
SB_BLOCK = 128
SB_SCALE = SB_HEAD_DIM ** -0.5
N_EXPERTS = 16
N_EXPERT_GROUPS = 4
EXPERTS_PER_GROUP = N_EXPERTS // N_EXPERT_GROUPS
TOP_K = 2
D_EXPERT = 512

kernel_name = 'yoco_ssd_stickbreak_moe_trunk'

def layer_norm(x, g, b):
    xf = x.astype(jnp.float32)
    mu = jnp.mean(xf, -1, keepdims=True)
    var = jnp.mean(jnp.square(xf - mu), -1, keepdims=True)
    y = (xf - mu) * lax.rsqrt(var + LN_EPS)
    return (y * g.astype(jnp.float32) + b.astype(jnp.float32)).astype(x.dtype)

def causal_depthwise_conv(x, w, bias):
    y = lax.conv_general_dilated(x, w[:, None, :].astype(x.dtype), window_strides=(1,),
                                 padding=[(CONV_WIDTH - 1, 0)],
                                 dimension_numbers=('NWC', 'WIO', 'NWC'),
                                 feature_group_count=x.shape[-1])
    return y + bias.astype(x.dtype)

def ssd_chunked(x, a, bm, cm):
    bsz, L = x.shape[:2]
    pad = (-L) % SSD_CHUNK
    x = jnp.pad(x, ((0, 0), (pad, 0), (0, 0), (0, 0)))
    a = jnp.pad(a, ((0, 0), (pad, 0), (0, 0)))
    bm = jnp.pad(bm, ((0, 0), (pad, 0), (0, 0), (0, 0)))
    cm = jnp.pad(cm, ((0, 0), (pad, 0), (0, 0), (0, 0)))
    nc = (L + pad) // SSD_CHUNK
    x = x.reshape(bsz, nc, SSD_CHUNK, SSM_GROUPS, SSM_HPG, SSM_HEAD_DIM)
    a = a.reshape(bsz, nc, SSD_CHUNK, SSM_GROUPS, SSM_HPG).transpose(0, 3, 4, 1, 2)
    bm = bm.reshape(bsz, nc, SSD_CHUNK, SSM_GROUPS, D_STATE)
    cm = cm.reshape(bsz, nc, SSD_CHUNK, SSM_GROUPS, D_STATE)
    a_cum = jnp.cumsum(a, axis=-1)
    causal = jnp.tril(jnp.ones((SSD_CHUNK, SSD_CHUNK), dtype=bool))
    seg = jnp.where(causal, a_cum[..., :, None] - a_cum[..., None, :], -jnp.inf)
    decay_ls = jnp.exp(seg)
    cb = jnp.einsum('bclgn,bcsgn->bgcls', cm, bm)
    y_diag = jnp.einsum('bgcls,bgrcls,bcsgrp->bclgrp', cb, decay_ls, x)
    decay_to_end = jnp.exp(a_cum[..., -1:] - a_cum)
    chunk_states = jnp.einsum('bclgn,bgrcl,bclgrp->cbgrpn', bm, decay_to_end, x)
    chunk_decay = jnp.exp(a_cum[..., -1]).transpose(3, 0, 1, 2)

    def carry_state(state, inp):
        st, dec = inp
        return state * dec[..., None, None] + st, state

    _, states_in = lax.scan(carry_state, jnp.zeros(chunk_states.shape[1:], jnp.float32),
                            (chunk_states, chunk_decay))
    y_off = jnp.einsum('bclgn,cbgrpn,bgrcl->bclgrp', cm, states_in, jnp.exp(a_cum))
    y = (y_diag + y_off).reshape(bsz, nc * SSD_CHUNK, SSM_HEADS, SSM_HEAD_DIM)
    return y[:, pad:]

def mamba2_mixer(h, w_in, conv_w, conv_b, dt_bias, a_log, d_skip, norm_w, w_out):
    bsz, L, _ = h.shape
    f32 = jnp.float32
    proj = h @ w_in
    z = proj[..., :D_INNER]
    xbc = jax.nn.silu(causal_depthwise_conv(proj[..., D_INNER:D_INNER + CONV_DIM], conv_w, conv_b))
    dt = jax.nn.softplus(proj[..., D_INNER + CONV_DIM:].astype(f32) + dt_bias.astype(f32))
    gn = SSM_GROUPS * D_STATE
    xs = xbc[..., :D_INNER].reshape(bsz, L, SSM_HEADS, SSM_HEAD_DIM).astype(f32)
    bm = xbc[..., D_INNER:D_INNER + gn].reshape(bsz, L, SSM_GROUPS, D_STATE).astype(f32)
    cm = xbc[..., D_INNER + gn:].reshape(bsz, L, SSM_GROUPS, D_STATE).astype(f32)
    a_neg = -jnp.exp(a_log.astype(f32))
    y = ssd_chunked(xs * dt[..., None], dt * a_neg, bm, cm)
    y = y + d_skip.astype(f32)[:, None] * xs
    y = y.reshape(bsz, L, D_INNER) * jax.nn.silu(z.astype(f32))
    yg = y.reshape(bsz, L, SSM_GROUPS, D_INNER // SSM_GROUPS)
    yg = yg * lax.rsqrt(jnp.mean(jnp.square(yg), -1, keepdims=True) + LN_EPS)
    y = yg.reshape(bsz, L, D_INNER) * norm_w.astype(f32)
    return y.astype(h.dtype) @ w_out

def shared_kv(h, w_k, w_v):
    bsz, L, _ = h.shape
    pad = (-L) % SB_BLOCK

    def heads(t):
        t = t.reshape(bsz, L, SB_HEADS, SB_HEAD_DIM).transpose(0, 2, 1, 3)
        return jnp.pad(t, ((0, 0), (0, 0), (pad, 0), (0, 0)))

    return heads(h @ w_k), heads(h @ w_v)

def stick_breaking_attention(h, w_q, w_o, k, v):
    bsz, L, _ = h.shape
    pad = (-L) % SB_BLOCK
    lp = L + pad
    nb = lp // SB_BLOCK
    q = (h @ w_q).reshape(bsz, L, SB_HEADS, SB_HEAD_DIM)
    q = jnp.pad(q, ((0, 0), (pad, 0), (0, 0), (0, 0)))
    q = q.reshape(bsz, nb, SB_BLOCK, SB_HEADS, SB_HEAD_DIM).transpose(1, 0, 3, 2, 4)
    kpos = jnp.arange(lp)

    def query_block(args):
        qb, blk = args
        z = jnp.einsum('bhqd,bhkd->bhqk', qb, k).astype(jnp.float32) * SB_SCALE
        qpos = blk * SB_BLOCK + jnp.arange(SB_BLOCK)
        mask = (kpos[None, :] < qpos[:, None]) & (kpos[None, :] >= pad)
        log_beta = jax.nn.log_sigmoid(z)
        log_keep = jnp.where(mask, jax.nn.log_sigmoid(-z), 0.0)
        later = lax.cumsum(log_keep, axis=3, reverse=True) - log_keep
        w = jnp.where(mask, jnp.exp(log_beta + later), 0.0)
        return jnp.einsum('bhqk,bhkd->bhqd', w.astype(v.dtype), v)

    o = lax.map(query_block, (q, jnp.arange(nb)))
    o = o.transpose(1, 0, 3, 2, 4).reshape(bsz, lp, SB_WIDTH)[:, pad:]
    return o @ w_o

def routed_moe(h, router_w, router_b, w_gate, w_up, w_down):
    bsz, L, d = h.shape
    xt = h.reshape(-1, d)
    logits = (xt @ router_w).astype(jnp.float32) + router_b.astype(jnp.float32)
    probs = jax.nn.softmax(logits, axis=-1)
    pg = probs.reshape(-1, N_EXPERT_GROUPS, EXPERTS_PER_GROUP)
    group_score = lax.top_k(pg, TOP_K)[0].sum(-1)
    gsel = jnp.argmax(group_score, axis=-1)
    p_in = jnp.take_along_axis(pg, gsel[:, None, None], axis=1)[:, 0]
    vals, idx = lax.top_k(p_in, TOP_K)
    eid = gsel[:, None] * EXPERTS_PER_GROUP + idx
    gates = vals / jnp.sum(vals, -1, keepdims=True)
    dense_gate = jnp.sum(jax.nn.one_hot(eid, N_EXPERTS, dtype=jnp.float32) * gates[..., None], axis=1)
    hid = jax.nn.silu(jnp.einsum('nd,edf->nef', xt, w_gate)) * jnp.einsum('nd,edf->nef', xt, w_up)
    hid = hid * dense_gate[..., None].astype(hid.dtype)
    out = jnp.einsum('nef,efd->nd', hid, w_down)
    return out.reshape(bsz, L, d)

def setup_inputs(seed: int = 0) -> dict:
    key = jax.random.key(seed)
    ks = iter(jax.random.split(key, 32))
    f32 = jnp.float32

    def nrm(shape, scale):
        return scale * jax.random.normal(next(ks), shape, f32)

    x = nrm((BATCH, SEQ, D_MODEL), 1.0)
    meta_tokens = nrm((N_META, D_MODEL), 1.0)
    mamba_w_in = nrm((N_A_LAYERS, D_MODEL, IN_DIM), D_MODEL ** -0.5)
    mamba_conv_w = nrm((N_A_LAYERS, CONV_WIDTH, CONV_DIM), CONV_WIDTH ** -0.5)
    mamba_conv_b = nrm((N_A_LAYERS, CONV_DIM), 0.02)
    dt0 = jnp.exp(jax.random.uniform(next(ks), (N_A_LAYERS, SSM_HEADS), f32, math.log(1e-3), math.log(1e-1)))
    mamba_dt_bias = dt0 + jnp.log(-jnp.expm1(-dt0))
    mamba_a_log = jnp.log(jax.random.uniform(next(ks), (N_A_LAYERS, SSM_HEADS), f32, 1.0, 16.0))
    mamba_d_skip = 1.0 + nrm((N_A_LAYERS, SSM_HEADS), 0.1)
    mamba_norm_w = 1.0 + nrm((N_A_LAYERS, D_INNER), 0.02)
    mamba_w_out = nrm((N_A_LAYERS, D_INNER, D_MODEL), BETA * D_INNER ** -0.5)
    sb_w_q = nrm((N_B_LAYERS, D_MODEL, SB_WIDTH), D_MODEL ** -0.5)
    sb_w_o = nrm((N_B_LAYERS, SB_WIDTH, D_MODEL), BETA * SB_WIDTH ** -0.5)
    shared_w_k = nrm((D_MODEL, SB_WIDTH), D_MODEL ** -0.5)
    shared_w_v = nrm((D_MODEL, SB_WIDTH), BETA * D_MODEL ** -0.5)
    ln_mix_g = 1.0 + nrm((DEPTH, D_MODEL), 0.02)
    ln_mix_b = nrm((DEPTH, D_MODEL), 0.02)
    ln_ffn_g = 1.0 + nrm((DEPTH, D_MODEL), 0.02)
    ln_ffn_b = nrm((DEPTH, D_MODEL), 0.02)
    router_w = nrm((D_MODEL, N_EXPERTS), D_MODEL ** -0.5)
    router_b = nrm((N_EXPERTS,), 0.01)
    moe_w_gate = nrm((DEPTH, N_EXPERTS, D_MODEL, D_EXPERT), D_MODEL ** -0.5)
    moe_w_up = nrm((DEPTH, N_EXPERTS, D_MODEL, D_EXPERT), D_MODEL ** -0.5)
    moe_w_down = nrm((DEPTH, N_EXPERTS, D_EXPERT, D_MODEL), BETA * D_EXPERT ** -0.5)
    return {'x': x, 'meta_tokens': meta_tokens, 'mamba_w_in': mamba_w_in,
            'mamba_conv_w': mamba_conv_w, 'mamba_conv_b': mamba_conv_b,
            'mamba_dt_bias': mamba_dt_bias, 'mamba_a_log': mamba_a_log,
            'mamba_d_skip': mamba_d_skip, 'mamba_norm_w': mamba_norm_w,
            'mamba_w_out': mamba_w_out, 'sb_w_q': sb_w_q, 'sb_w_o': sb_w_o,
            'shared_w_k': shared_w_k, 'shared_w_v': shared_w_v,
            'ln_mix_g': ln_mix_g, 'ln_mix_b': ln_mix_b, 'ln_ffn_g': ln_ffn_g,
            'ln_ffn_b': ln_ffn_b, 'router_w': router_w, 'router_b': router_b,
            'moe_w_gate': moe_w_gate, 'moe_w_up': moe_w_up, 'moe_w_down': moe_w_down}

def reference(x, meta_tokens, mamba_w_in, mamba_conv_w, mamba_conv_b, mamba_dt_bias,
              mamba_a_log, mamba_d_skip, mamba_norm_w, mamba_w_out, sb_w_q, sb_w_o,
              shared_w_k, shared_w_v, ln_mix_g, ln_mix_b, ln_ffn_g, ln_ffn_b,
              router_w, router_b, moe_w_gate, moe_w_up, moe_w_down):
    bsz = x.shape[0]
    meta = jnp.broadcast_to(meta_tokens.astype(x.dtype)[None], (bsz, N_META, D_MODEL))
    h = jnp.concatenate([meta, x], axis=1)
    for layer in range(DEPTH):
        if layer == N_A_LAYERS:
            k_sh, v_sh = shared_kv(h, shared_w_k, shared_w_v)
        if layer < N_A_LAYERS:
            i = layer
            mix = mamba2_mixer(h, mamba_w_in[i], mamba_conv_w[i], mamba_conv_b[i], mamba_dt_bias[i],
                               mamba_a_log[i], mamba_d_skip[i], mamba_norm_w[i], mamba_w_out[i])
        else:
            j = layer - N_A_LAYERS
            mix = stick_breaking_attention(h, sb_w_q[j], sb_w_o[j], k_sh, v_sh)
        h = layer_norm(ALPHA * h + mix, ln_mix_g[layer], ln_mix_b[layer])
        ffn = routed_moe(h, router_w, router_b, moe_w_gate[layer], moe_w_up[layer], moe_w_down[layer])
        h = layer_norm(ALPHA * h + ffn, ln_ffn_g[layer], ln_ffn_b[layer])
    return h[:, N_META:]


_drawn_inputs = setup_inputs


def setup_inputs(seed=0):
    import zlib

    import numpy as np

    out = dict(_drawn_inputs(seed))
    spreads = {}
    factors = {}
    for name, (base, spread) in spreads.items():
        noise = np.random.default_rng([zlib.crc32(name.encode()), seed]).standard_normal(out[name].shape)
        drawn = base * np.exp(spread * noise) if base else spread * noise
        out[name] = __import__('jax').numpy.asarray(drawn.astype(out[name].dtype))
    for name, factor in factors.items():
        out[name] = (out[name] * factor).astype(out[name].dtype)
    return out
```

```python
from contextlib import ExitStack

import concourse.bass as bass
from concourse import mybir

F32 = mybir.dt.float32
I32 = mybir.dt.int32
ALU = mybir.AluOpType
ACT = mybir.ActivationFunctionType
AX = mybir.AxisListType

P = 128
D_MODEL = 1024
KD = D_MODEL // P
META = 16
SEQ = 256
L = META + SEQ
TILES = [(0, META), (META, P), (META + P, P)]
DEPTH = 2
ALPHA = (2.0 * DEPTH) ** 0.25
EPS = 1e-5
TOP = 40.0
HEADS = 32
HD = 64
GROUPS = 4
HPG = HEADS // GROUPS
D_INNER = HEADS * HD
KI = D_INNER // P
CONV_TILES = KI + 2 * GROUPS
CONV_W = 4
SB_HEADS = 16
N_EXP = 16
N_GRP = 4
PER_GRP = N_EXP // N_GRP
D_EXP = 512
CAP = 64
NEVER = 1e6
PAIRS = N_EXP // 2
PICKS = PAIRS + 1
UNIT = 4096
RING = 6


class Link:

    def __init__(self, eng, sem):
        self.eng, self.sem, self.n = eng, sem, 0

    def __call__(self, ins):
        self.n += 1
        ins.then_inc(self.sem, 1)
        self.eng.wait_ge(self.sem, self.n)


def build_trunk(nc, x, meta_tokens, mamba_w_in, mamba_conv_w, mamba_conv_b, mamba_dt_bias,
                mamba_a_log, mamba_d_skip, mamba_norm_w, mamba_w_out, sb_w_q, sb_w_o,
                shared_w_k, shared_w_v, ln_mix_g, ln_mix_b, ln_ffn_g, ln_ffn_b,
                router_w, router_b, moe_w_gate, moe_w_up, moe_w_down, out, stop="", step=CAP):
    cap = CAP
    MAX_ROUNDS = -(-L // step)
    ctx = ExitStack()
    with ctx:
        def sb(name, shape, dt=F32):
            return ctx.enter_context(nc.sbuf_tensor(name, shape, dt))

        def sem(name):
            return ctx.enter_context(nc.semaphore(name))

        ps = ctx.enter_context(nc.psum_tensor("ps", [P, 8, 512], F32))
        ring = sb("ring", [P, RING, UNIT])
        hT = sb("hT", [P, KD, L])
        rT = sb("rT", [P, KD, L])
        tok = sb("tok", [P, 3, D_MODEL])
        ident = sb("ident", [P, P])
        upto = sb("upto", [P, P])
        after = sb("after", [P, P])
        before = sb("before", [P, P])
        negfrom = sb("negfrom", [P, P])
        ones = sb("ones", [P, P])
        negones = sb("negones", [P, P])
        negfrom0 = sb("negfrom0", [64, 64])
        never = sb("never", [P, P])
        mean_model = sb("mean_model", [P, P])
        mean_group = sb("mean_group", [P, P])
        slots = sb("slots", [P, cap])
        par1 = sb("par1", [P, 120])
        par2 = sb("par2", [P, 80])
        prow = sb("prow", [P, 2, P])
        dskip = sb("dskip", [P, KI])
        dtb = sb("dtb", [HEADS, 1])
        alog = sb("alog", [HEADS, 1])
        rbias = sb("rbias", [N_EXP, 1])
        epsc = sb("epsc", [P, 1])
        wdt = sb("wdt", [P, KD, HEADS])
        rw = sb("rw", [P, KD, N_EXP])
        logit = sb("logit", [N_EXP, L])
        route = sb("route", [P, 12, 3 * N_EXP])
        cmpb = sb("cmpb", [P, 3, 3 * N_EXP * PER_GRP])
        lower = sb("lower", [P, PER_GRP, PER_GRP])
        higher = sb("higher", [P, PER_GRP, PER_GRP])
        rank = sb("rank", [P, 3, N_EXP + 2])
        gate = sb("gate", [P, 3, N_EXP + 2])
        rmax = sb("rmax", [P, 4])
        extra = sb("extra", [1, 1], I32)
        PHASE = 15616
        phase = sb("phase", [P, PHASE])

        def carver():
            at = [0]

            def take(*shape, rows=P):
                n = 1
                for s in shape:
                    n *= s
                assert at[0] + n <= PHASE, at[0] + n
                v = phase[0:rows, at[0]:at[0] + n]
                at[0] += n
                if len(shape) == 2:
                    v = v.rearrange("p (a b) -> p a b", a=shape[0])
                if len(shape) == 3:
                    v = v.rearrange("p (a b c) -> p a b c", a=shape[0], b=shape[1])
                return v
            return take

        take = carver()
        zT = take(KI, L)
        xsT = take(KI, L)
        bcT = take(2 * GROUPS, L)
        xdt = take(HEADS, HD)
        state = take(HEADS, HD)
        convw = state.rearrange("p a b -> p (a b)")[:, 0:3 * L].rearrange("p (a b) -> p a b", a=3)
        tok_f = tok[:, :, :].rearrange("p a b -> p (a b)")
        decay = tok_f[:, 0:2048].rearrange("p (s h l) -> p s h l", s=2, h=HPG)
        xde = tok_f[:, 2048:2560].rearrange("p (h d) -> p h d", h=HPG)
        cbm = tok_f[:, 2560:2688]
        lastd = tok_f[:, 2688:2704].rearrange("p (s h) -> p s h", s=2)
        rT_f = rT[:, :, :].rearrange("p a b -> p (a b)")
        cdec = rT_f[:, 0:1024].rearrange("p (h l) -> p h l", h=HPG)
        btok = rT_f[:, 1024:2048].rearrange("p (t n) -> p t n", t=2)
        def squares(grp):
            return xsT[:, 4 * grp:4 * grp + 4, :]

        def rms(grp, inv):
            return bcT[:, GROUPS * inv + grp, :]

        dtv = [zT[0:HEADS, n, :] for n in range(10)]
        daT = zT[0:2 * HEADS, 10, :]
        acT = sb("acT", [HEADS, L])
        da = sb("da", [P, 3, 2 * HEADS])
        dte = sb("dte", [P, 3, HEADS])
        acum = sb("acum", [P, 3, HEADS])
        take = carver()
        sq = take(KD, L)
        xg = take(KD, 2 * cap)
        sg = take(256)
        hid = take(256)
        hidT = take(2, 2 * cap)
        ysb = take(2, 512)
        pick = take(3, 2 * cap)
        give = take(2, 3, 2 * cap)
        giveT = take(2, L)
        stat = take(2, L)
        take = carver()
        kT = take(KD, L)
        qT = take(KD, SEQ)
        oT = take(KD, SEQ)
        soft = take(2, 1024)
        wts = take(2, 1024)
        kz = take(KD, 64)
        vz = take(KD, P, rows=64)
        vtok = tok

        s_const = sem("s_const")
        s_xin = sem("s_xin")
        s_par = sem("s_par")
        s_par2 = sem("s_par2")
        s_wsm = sem("s_wsm")
        s_cstep = sem("s_cstep")
        s_dve = sem("s_dve")
        s_act = sem("s_act")
        s_ready0 = sem("s_ready0")
        s_skip = sem("s_skip")
        s_rw = sem("s_rw")

        class Ring:

            def __init__(self, name):
                self.full = [sem(f"{name}_full{s}") for s in range(RING)]

        def cols(w, lo, hi):
            return w[:, lo:hi].rearrange("(k p) f -> p k f", p=P)

        w_in, w_out = mamba_w_in[0], mamba_w_out[0]
        in_units = [8, 9, 4, 5, 6, 7, 0, 1, 2, 3]
        mamba_units = [cols(w_in, 512 * u, 512 * u + 512) for u in in_units] + \
                      [cols(w_out, 256 * u, 256 * u + 256) for u in range(4)]
        attn_units = [cols(w, 512 * u, 512 * u + 512)
                      for w in (shared_w_k, sb_w_q[0], shared_w_v, sb_w_o[0]) for u in range(2)]
        R_M, R_A = Ring("rm"), Ring("ra")
        BASE_M = 0
        BASE_E1 = 3
        BASE_A = 3
        BASE_E2 = 0

        def unit(base, n):
            return ring[:, (base + n) % RING, :]

        def fills(base, n):
            return 16 * (n // RING + 1)

        class Path:
            def __init__(self, tag):
                self.full = [sem(f"{tag}_full{s}") for s in range(RING)]
                self.pick_ready = sem(f"{tag}_pick_ready")
                self.gathered = sem(f"{tag}_gathered")
                self.xg_ready = sem(f"{tag}_xg_ready")
                self.give_ready = sem(f"{tag}_give_ready")
                self.give_turned = sem(f"{tag}_give_turned")
                self.giveT_ready = sem(f"{tag}_giveT_ready")
                self.up_done = sem(f"{tag}_up_done")
                self.silu_done = sem(f"{tag}_silu_done")
                self.hid_ready = sem(f"{tag}_hid_ready")
                self.hid_turned = sem(f"{tag}_hid_turned")
                self.hidT_ready = sem(f"{tag}_hidT_ready")
                self.down_done = sem(f"{tag}_down_done")
                self.y_ready = sem(f"{tag}_y_ready")
                self.spread = sem(f"{tag}_spread")
                self.added = sem(f"{tag}_added")

        first_path, further_path = Path("first"), Path("further")
        BASE_E = [BASE_E1, BASE_E2]
        s_ranked = sem("s_ranked")
        s_router = sem("s_router")
        s_logit = sem("s_logit")
        s_turned = sem("s_turned")
        s_below = sem("s_below")
        s_numer = sem("s_numer")
        s_chosen = sem("s_chosen")
        s_counted = sem("s_counted")
        s_routed = sem("s_routed")
        s_htok_ps = sem("s_htok_ps")
        s_htok = sem("s_htok")
        htok_before = [0, 6]
        s_lnx = sem("s_lnx")
        s_lnm = sem("s_lnm")
        s_lnc = sem("s_lnc")
        s_lnq = sem("s_lnq")
        s_lnv = sem("s_lnv")
        s_lns = sem("s_lns")
        s_lnn = sem("s_lnn")
        s_ln = sem("s_ln")
        names = ("tin", "tin_e", "ptr", "ptr_e", "acr", "proj", "conv_done", "xbc", "z_read", "dtx", "dtn", "dte_e",
                 "dtea", "da_t", "daT_r", "da_r", "acp", "acs", "dte_x", "bt", "btok", "xtr", "xdt", "bc",
                 "cb", "cbm", "dd", "expd", "expc", "mt", "cs", "yps", "yadd", "xde", "stps", "stup",
                 "zsilu", "yz", "rsq", "rps", "rsd", "yn", "outp", "outr")
        m = {n: sem(f"m_{n}") for n in names}
        anames = ("kq", "kq_e", "v", "v_e", "blocks", "vz", "z", "bound", "e", "ln", "sp", "arg", "w", "o", "o_e",
                  "outp", "outr", "fin", "fin_e", "store")
        a = {n: sem(f"a_{n}") for n in anames}

        rnd_tokens = [TILES, TILES[1:]]
        C0 = [0, META]

        def tiles_of(layer):
            return [(t, o, n) for t, (o, n) in enumerate(TILES) if t >= layer]

        block = ctx.enter_context(nc.Block())

        @block.gpsimd
        def _(pool):
            g = nc.gpsimd
            for n, (t, v) in enumerate(((ident, 1.0), (upto, 1.0), (after, 1.0), (before, 1.0),
                                        (negfrom, -1.0), (lower, 1.0), (higher, 1.0), (never, -1e30))):
                g.memset(t[:], v).then_inc(s_cstep, 1)
            g.memset(negfrom0[:], 0.0).then_inc(s_cstep, 1)
            g.memset(epsc[:], EPS).then_inc(s_cstep, 1)
            g.memset(ones[:], 1.0).then_inc(s_cstep, 1)
            g.memset(negones[:], -1.0).then_inc(s_cstep, 1)
            g.memset(mean_model[:], 1.0 / D_MODEL).then_inc(s_cstep, 1)
            g.memset(mean_group[:], 1.0 * GROUPS / D_INNER).then_inc(s_cstep, 1)
            pool.wait_ge(s_cstep, 14)

            def select(t, op, cm, pattern):
                g.affine_select(out=t, in_=t, compare_op=op, fill=0.0, base=0, pattern=pattern,
                                channel_multiplier=cm).then_inc(s_const, 1)

            select(ident[:], ALU.is_equal, 1, [[-1, P]])
            select(upto[:], ALU.is_ge, -1, [[1, P]])
            select(after[:], ALU.is_gt, 1, [[-1, P]])
            select(before[:], ALU.is_gt, -1, [[1, P]])
            select(negfrom[:], ALU.is_ge, 1, [[-1, P]])
            select(lower[:], ALU.is_gt, 0, [[1, PER_GRP], [-1, PER_GRP]])
            select(higher[:], ALU.is_gt, 0, [[-1, PER_GRP], [1, PER_GRP]])
            select(never[:], ALU.is_ge, 1, [[-1, P]])
            g.iota(slots[:], [[1, cap]], base=0, channel_multiplier=0,
                   allow_small_or_imprecise_dtypes=True).then_inc(s_const, 1)
            pool.wait_ge(s_const, 9)
            g.tensor_copy(negfrom0[0:META, 0:META], negfrom[0:META, 0:META])
            if step < cap:
                g.memset(slots[:, step:cap], NEVER).then_inc(s_cstep, 1)
                pool.wait_ge(s_cstep, 15)
            g.tensor_copy(negfrom0[32:32 + META, 32:32 + META], negfrom[0:META, 0:META]).then_inc(s_const, 1)
            for q in range(3 * GROUPS):
                t, grp = divmod(q, GROUPS)
                n = TILES[t][1]
                if t < 2:
                    pool.wait_ge(m["xdt"], q + 1)
                    if q == 0:
                        pool.wait_ge(m["dte_x"], 3)
                    else:
                        pool.wait_ge(m["stps"], q)
                    g.tensor_tensor(xde[0:n], xdt[0:n, grp * HPG:(grp + 1) * HPG, :],
                                    dte[0:n, t, grp * HPG:(grp + 1) * HPG].unsqueeze(2).broadcast_to([n, HPG, HD]),
                                    ALU.mult).then_inc(m["xde"], 1)
                pool.wait_ge(m["cbm"], q + 1)
                pool.wait_ge(m["expd"], q + 1)
                d = decay[0:n, q % 2, :, 0:n]
                g.tensor_tensor(d, d, cbm[0:n, 0:n].unsqueeze(1).broadcast_to([n, HPG, n]),
                                ALU.mult).then_inc(m["mt"], 1)

        @block.sync
        def _(sp):
            def send(sem_, base, n, src):
                dst = unit(base, n)
                if len(src.shape) == 3:
                    dst = dst.rearrange("p (a b) -> p a b", a=src.shape[1])
                sp.dma_start(dst, src).then_inc(sem_, 16)

            sp.dma_start(tok[0:META, 0, :], meta_tokens).then_inc(s_xin, 16)
            for t in (1, 2):
                sp.dma_start(tok[:, t, :], x[0, (t - 1) * P:t * P, :]).then_inc(s_xin, 16)
            sp.dma_start(wdt[:], cols(w_in, 5120, 5152)).then_inc(s_wsm, 16)
            for n, src in enumerate(mamba_units):
                if n == 1:
                    sp.dma_start(prow[0:16, 1, :], mamba_norm_w[0].rearrange("(c p) -> c p", p=P))\
                        .then_inc(s_par2, 16)
                    for r, v in enumerate((ln_mix_g, ln_mix_b, ln_ffn_g, ln_ffn_b)):
                        sp.dma_start(prow[16 + 16 * r:32 + 16 * r, 1, :], v.rearrange("l (c p) -> (l c) p", p=P))\
                            .then_inc(s_par2, 16)
                    sp.wait_ge(s_par, 32)
                    sp.wait_ge(s_ready0, 32)
                if n == 3:
                    dsk = mamba_d_skip.rearrange("o (t two) -> o two t", two=2)
                    for par in range(2):
                        sp.dma_start(dskip[par * 64:par * 64 + 64, :], dsk[:, par, :].broadcast_to([64, KI]),
                                     allow_slow_non_contiguous=True).then_inc(s_skip, 16)
                    sp.dma_start(rbias[:], router_b.rearrange("(e o) -> e o", o=1)).then_inc(s_rw, 16)
                    sp.dma_start(rw[:], router_w.rearrange("(k p) e -> p k e", p=P)).then_inc(s_rw, 16)
                if n >= RING:
                    sp.wait_ge(m["proj"], 1 + 4 * (n - RING + 1))
                if n >= 10:
                    dst = unit(BASE_M, n).rearrange("p (a b) -> p a b", a=KI)
                    sp.dma_start(dst, src).then_inc(R_M.full[(BASE_M + n) % RING], 16)
                else:
                    send(R_M.full[(BASE_M + n) % RING], BASE_M, n, src)

            def send_expert(p, layer, e, k, before=()):
                for j, w in enumerate((moe_w_gate[layer], moe_w_up[layer], moe_w_down[layer])):
                    if before:
                        sp.wait_ge(*before[j])
                    dst = unit(BASE_E[layer], 3 * k + j).rearrange("p (a b) -> p a b", a=w.shape[1] // P)
                    src = w[bass.ds(e, 1)].rearrange("o (a p) f -> p (o a) f", p=P)
                    sp.dma_start(dst, src).then_inc(p.full[(BASE_E[layer] + 3 * k + j) % RING], 16)

            def send_pair(p, layer, i, q):
                for k in range(2):
                    up, down = (p.up_done, 2 * q + k - 1), (p.down_done, 2 * q + k - 1)
                    send_expert(p, layer, 2 * i + k, k, (up, up, down))

            def moe_stream(layer, before, rounds_before):
                p, r = first_path, further_path
                for k in range(2):
                    send_expert(p, layer, k, k, before[3 * k:3 * k + 3])
                with sp.Fori(1, PAIRS) as i:
                    send_pair(p, layer, i, layer * PAIRS + i)
                sp.wait_ge(s_routed, layer + 1)
                further = sp.value_load(extra[0:1, 0:1], min_val=0, max_val=MAX_ROUNDS - 1)
                with sp.If(further > 0):
                    with sp.Fori(0, further) as rr:
                        done = sp.snap(rounds_before + rr)
                        sp.wait_ge(s_ranked, done + 1)
                        for k in range(2):
                            send_expert(r, layer, k, k)
                        with sp.Fori(1, PAIRS) as i:
                            send_pair(r, layer, i, done * PAIRS + i)
                    sp.wait_ge(s_lnm, 2 * layer + 2)
                return further

            if stop == "mamba":
                return
            op = m["outp"]
            further = moe_stream(0, ((m["proj"], 41), (op, 2), (op, 4), (op, 6), (op, 8), (m["proj"], 37)), 0)
            if stop == "moe0":
                return
            pf = first_path
            free = [(pf.up_done, 15), (pf.up_done, 15), (pf.down_done, 15),
                    (pf.up_done, 16), (pf.up_done, 16), (pf.down_done, 16), (a["kq"], 4), (a["kq"], 8)]
            for n, src in enumerate(attn_units):
                sp.wait_ge(*free[n])
                send(R_A.full[(BASE_A + n) % RING], BASE_A, n, src)
            if stop == "attn":
                return
            moe_stream(1, ((a["kq"], 16), (a["v"], 3), (a["v"], 6), (a["outp"], 4), (a["outp"], 8), (a["kq"], 12)),
                       further)

        @block.tensor
        def _(pe):
            mm = nc.tensor.matmul
            tr = nc.tensor.transpose
            pe.wait_ge(s_const, 10)
            pe.wait_ge(s_xin, 48)
            for g6 in range(6):
                t, half = divmod(g6, 2)
                n = TILES[t][1]
                if g6 >= 4:
                    pe.wait_ge(m["tin_e"], g6 - 3)
                for k in range(4):
                    kk = 4 * half + k
                    last = tr(ps[:, g6 % 4, k * P:k * P + n], tok[0:n, t, kk * P:(kk + 1) * P], ident[0:n, 0:n])
                last.then_inc(m["tin"], 1)
            pe.wait_ge(s_par, 32)
            tr(ps[:, 4, 0:120], prow[0:120, 0, :], ident[0:120, 0:120]).then_inc(m["ptr"], 1)
            pe.wait_ge(m["tin_e"], 6)
            pe.wait_ge(s_wsm, 16)
            for k in range(KD):
                last = mm(ps[0:HEADS, 0, 0:L], wdt[:, k, :], hT[:, k, :], start=(k == 0), stop=(k == KD - 1))
            last.then_inc(m["proj"], 1)

            def project(n_unit, j, bank):
                w = unit(BASE_M, n_unit).rearrange("p (k f) -> p k f", k=KD)
                if j == 0:
                    pe.wait_ge(R_M.full[(BASE_M + n_unit) % RING], fills(BASE_M, n_unit))
                for k in range(KD):
                    last = mm(ps[:, bank, 0:L], w[:, k, j * P:(j + 1) * P], hT[:, k, :],
                              start=(k == 0), stop=(k == KD - 1))
                last.then_inc(m["proj"], 1)
                return last

            def add_mean(i, k):
                c0 = C0[i // 2]
                if i % 2 == 0:
                    pe.wait_ge(s_lnx, KD * (i // 2) + k + 1)
                ins = mm(ps[:, 0, c0:L], mean_model[:, :], rT[:, k, c0:L], start=(k == 0), stop=(k == KD - 1))
                if k == KD - 1:
                    ins.then_inc(s_lnm, 1)

            def layer_norm(i):
                c0 = C0[i // 2]
                for k in range(KD - 1 if i % 2 == 0 else 0, KD):
                    add_mean(i, k)
                for k in range(KD):
                    if k % 2 == 0:
                        pe.wait_ge(s_lnq, 4 * i + k // 2 + 1)
                    last = mm(ps[:, 1, c0:L], mean_model[:, :], sq[:, k, c0:L], start=(k == 0), stop=(k == KD - 1))
                last.then_inc(s_lnv, 1)

            for c in range(CONV_TILES):
                if c >= 3:
                    pe.wait_ge(m["conv_done"], c - 2)
                project(c // 4, c % 4, 1 + c % 3)
                if c == 4:
                    pe.wait_ge(s_par2, 16 * 5)
                    pe.wait_ge(m["ptr_e"], 1)
                    tr(ps[:, 4, 128:208], prow[0:80, 1, :], ident[0:80, 0:80]).then_inc(m["ptr"], 1)
                if c == 6:
                    pe.wait_ge(m["daT_r"], 1)
                    for t, (o, n) in enumerate(TILES):
                        last = tr(ps[0:n, 5, t * 64:t * 64 + 64], daT[:, o:o + n], ident[0:64, 0:64])
                    last.then_inc(m["da_t"], 1)
                if c == 10:
                    pe.wait_ge(m["da_r"], 3)
                    for t, (o, n) in enumerate(TILES):
                        a_t = da[0:n, t, HEADS:2 * HEADS]
                        mm(ps[0:n, 6, t * 32:t * 32 + 32], after[0:n, 0:n], a_t, start=True, stop=True)
                        mm(ps[0:n, 6, 96 + t * 32:128 + t * 32], upto[0:n, 0:n], a_t, start=True, stop=True)
                        last = mm(ps[0:HEADS, 7, o:o + n], a_t, upto[0:n, 0:n], start=True, stop=True)
                    last.then_inc(m["acp"], 1)
            pe.wait_ge(m["xbc"], CONV_TILES)
            pe.wait_ge(m["ptr_e"], 2)
            for t in range(2):
                o, n = TILES[t]
                for grp in range(GROUPS):
                    last = tr(ps[0:n, 4 + t, grp * P:(grp + 1) * P], bcT[:, grp, o:o + n], ident[:, :])
                last.then_inc(m["bt"], 1)

            def ssd_front(q):
                t, grp = divmod(q, GROUPS)
                o, n = TILES[t]
                if q == 0:
                    pe.wait_ge(m["dtx"], 1)
                else:
                    pe.wait_ge(m["xdt"], q)
                for k in range(4):
                    last = tr(ps[0:n, 0, k * P:(k + 1) * P], xsT[:, grp * 4 + k, o:o + n], ident[:, :])
                last.then_inc(m["xtr"], 1)
                if q == 0:
                    pe.wait_ge(m["acs"], 1)
                else:
                    pe.wait_ge(m["dd"], q)
                    if q > GROUPS:
                        pe.wait_ge(m["expc"], q - GROUPS)
                for h in range(HPG):
                    hh = grp * HPG + h
                    last = mm(ps[:, 2 + h // 4, (h % 4) * P:(h % 4) * P + n],
                              ident[0:HEADS, hh:hh + 1].broadcast_to([HEADS, P]), acT[:, o:o + n],
                              start=True, stop=True)
                last.then_inc(m["bc"], 1)
                if q > 0:
                    pe.wait_ge(m["cbm"], q)
                mm(ps[0:n, 1, 0:n], bcT[:, grp, o:o + n], bcT[:, GROUPS + grp, o:o + n],
                   start=True, stop=True).then_inc(m["cb"], 1)

            def ssd_back(q):
                t, grp = divmod(q, GROUPS)
                o, n = TILES[t]
                pe.wait_ge(m["mt"], q + 1)
                if t >= 1:
                    pe.wait_ge(m["cs"], q - GROUPS + 1)
                    pe.wait_ge(m["stup"], min(q - GROUPS + 1, 2 * GROUPS))
                if q > 0:
                    pe.wait_ge(m["yadd"], q)
                for h in range(HPG):
                    hh = grp * HPG + h
                    dst = ps[(h % 2) * HD:(h % 2) * HD + HD, 4, (h // 2) * P:(h // 2) * P + n]
                    last = mm(dst, xdt[0:n, hh, :], decay[0:n, q % 2, h, 0:n], start=True, stop=(t == 0))
                    if t >= 1:
                        last = mm(dst, state[:, hh, :], cdec[:, h, 0:n], start=False, stop=True)
                last.then_inc(m["yps"], 1)
                if t < 2:
                    pe.wait_ge(m["xde"], q + 1)
                    if q > 0:
                        pe.wait_ge(m["stup"], q)
                    if q == 0:
                        pe.wait_ge(m["btok"], 2)
                    mm(ps[:, 5, :], btok[0:n, t, grp * P:(grp + 1) * P], xde[0:n].rearrange("p h d -> p (h d)"),
                       start=True, stop=True).then_inc(m["stps"], 1)

            zt = 0

            def z_tile():
                nonlocal zt
                if zt < KI:
                    if zt == 0:
                        pe.wait_ge(m["dte_x"], 3)
                        pe.wait_ge(m["acr"], 3)
                    if zt >= 2:
                        pe.wait_ge(m["z_read"], zt - 1)
                    project(6 + zt // 4, zt % 4, 6 + zt % 2)
                    zt += 1

            pe.wait_ge(m["acs"], 1)
            for q in range(3 * GROUPS):
                if q == 0:
                    pe.wait_ge(m["btok"], 2)
                ssd_front(q)
                if q < 4:
                    z_tile()
                if q > 0:
                    ssd_back(q - 1)
                z_tile()
            ssd_back(3 * GROUPS - 1)
            for grp in range(GROUPS):
                pe.wait_ge(m["rsq"], grp + 1)
                if grp == 0:
                    pe.wait_ge(m["xdt"], 3 * GROUPS)
                    pe.wait_ge(m["dd"], 3 * GROUPS)
                    pe.wait_ge(m["cbm"], 3 * GROUPS)
                    pe.wait_ge(m["expc"], 2 * GROUPS)
                for k in range(4):
                    last = mm(ps[:, grp, 0:L], mean_group[:, :], squares(grp)[:, k, :], start=(k == 0), stop=(k == 3))
                last.then_inc(m["rps"], 1)
            pe.wait_ge(m["z_read"], KI)
            pe.wait_ge(m["yadd"], 3 * GROUPS)
            pe.wait_ge(m["stup"], 2 * GROUPS)
            w = unit(BASE_M, 10).rearrange("p (k f) -> p k f", k=KI)
            pe.wait_ge(R_M.full[(BASE_M + 10) % RING], fills(BASE_M, 10))
            for k in range(KI):
                pe.wait_ge(m["yn"], k + 1)
                for mt in range(2):
                    ins = mm(ps[:, 4 + mt, 0:L], w[:, k, mt * P:(mt + 1) * P], zT[:, k, :],
                             start=(k == 0), stop=(k == KI - 1))
                    if k == KI - 1:
                        ins.then_inc(m["outp"], 1)
            for mt in range(2, KD):
                n_unit = 10 + mt // 2
                w = unit(BASE_M, n_unit).rearrange("p (k f) -> p k f", k=KI)
                if mt % 2 == 0:
                    pe.wait_ge(R_M.full[(BASE_M + n_unit) % RING], fills(BASE_M, n_unit))
                if mt >= 4:
                    pe.wait_ge(s_lnx, mt - 3)
                for k in range(KI):
                    last = mm(ps[:, 4 + mt % 4, 0:L], w[:, k, (mt % 2) * P:(mt % 2 + 1) * P], zT[:, k, :],
                              start=(k == 0), stop=(k == KI - 1))
                last.then_inc(m["outp"], 1)
                for k in range(0 if mt == 2 else mt - 1, mt):
                    add_mean(0, k)

            layer_norm(0)

            def router(l):
                c0 = C0[l]
                i = 2 * l
                if l == 0:
                    pe.wait_ge(s_rw, 32)
                for k in range(KD):
                    pe.wait_ge(s_ln, KD * i + k + 1)
                    last = mm(ps[0:N_EXP, 2, c0:L], rw[:, k, :], hT[:, k, c0:L], start=(k == 0), stop=(k == KD - 1))
                last.then_inc(s_router, 1)
                g_ = 0
                for t, o, n in tiles_of(l):
                    for half in range(2):
                        if g_ >= 2:
                            pe.wait_ge(s_htok, htok_before[l] + g_ - 1)
                        for k in range(4):
                            last = tr(ps[0:n, 4 + g_ % 2, k * P:(k + 1) * P],
                                      hT[:, 4 * half + k, o:o + n], ident[:, :])
                        last.then_inc(s_htok_ps, 1)
                        g_ += 1
                pe.wait_ge(s_logit, l + 1)
                for t, o, n in tiles_of(l):
                    last = tr(ps[0:n, 3, t * N_EXP:(t + 1) * N_EXP], logit[:, o:o + n], ident[0:N_EXP, 0:N_EXP])
                last.then_inc(s_turned, 1)
                pe.wait_ge(s_chosen, l + 1)
                sel = route[:, 8, :].rearrange("p (t e) -> p t e", t=3)
                tl = tiles_of(l)
                for t, o, n in tl:
                    for t2, o2, n2 in tl:
                        if t2 <= t:
                            lhs = before[0:n, 0:n] if t2 == t else ones[0:n2, 0:n]
                            mm(ps[0:n, 2, t * N_EXP:(t + 1) * N_EXP], lhs, sel[0:n2, t2, :],
                               start=(t2 == tl[0][0]), stop=(t2 == t))
                for t, o, n in tl:
                    last = mm(ps[:, 2, 3 * N_EXP:4 * N_EXP], ones[0:n, :], sel[0:n, t, :],
                              start=(t == tl[0][0]), stop=(t == 2))
                last.then_inc(s_counted, 1)

            def moe_round(p, l, done):
                tl = tiles_of(l)
                c0 = C0[l]

                def slot(k, j):
                    return (BASE_E[l] + 3 * k + j) % RING

                def gather(i_next):
                    pe.wait_ge(p.pick_ready, done * PICKS + i_next + 1)
                    for k in range(KD):
                        for t, o, n in tl:
                            last = mm(ps[:, 4 + k // 4, (k % 4) * P:(k % 4) * P + 2 * cap],
                                      tok[0:n, t, k * P:(k + 1) * P], pick[0:n, t, :],
                                      start=(t == tl[0][0]), stop=(t == 2))
                    last.then_inc(p.gathered, 1)

                def up(q, k):
                    for j in range(2):
                        pe.wait_ge(p.full[slot(k, j)], 16 * q + 16)
                    s0 = slot(k, 0)
                    w = ring[:, s0:s0 + 2, :].rearrange("p g (k f) -> p g k f", k=KD)
                    for kk in range(KD):
                        for half in range(2):
                            last = mm(ps[half * 64:half * 64 + cap, 0, :], xg[:, kk, k * cap:(k + 1) * cap],
                                      w[:, :, kk, half * 256:half * 256 + 256],
                                      start=(kk == 0), stop=(kk == KD - 1))
                    last.then_inc(p.up_done, 1)

                def turn_hidden(x):
                    pe.wait_ge(p.hid_ready, x + 1)
                    for j in range(2):
                        last = tr(ps[:, 1, j * P:(j + 1) * P], hid[:, j * P:(j + 1) * P], ident[:, :])
                    last.then_inc(p.hid_turned, 1)

                def down(x, q, k):
                    if k == 1:
                        pe.wait_ge(p.y_ready, x)
                    pe.wait_ge(p.hidT_ready, x + 1)
                    pe.wait_ge(p.full[slot(k, 2)], 16 * q + 16)
                    w = ring[:, slot(k, 2), :].rearrange("p (b d) -> p b d", b=4)
                    for b in range(4):
                        for dh in range(2):
                            last = mm(ps[dh * 64:dh * 64 + cap, 2, :],
                                      hidT[:, b % 2, (b // 2) * 64:(b // 2) * 64 + cap],
                                      w[:, b, dh * 512:(dh + 1) * 512], start=(b == 0), stop=(b == 3))
                    last.then_inc(p.down_done, 1)

                def spread(q):
                    pe.wait_ge(p.giveT_ready, 2 * q + 2)
                    pe.wait_ge(p.y_ready, 2 * q + 2)
                    for s in range(4):
                        b0 = 6 if s % 2 == 0 else 2
                        if s >= 2:
                            pe.wait_ge(p.added, 4 * q + s - 1)
                        for k in range(2):
                            for half in range(2):
                                last = mm(ps[:, b0 + half, c0:L],
                                          ysb[half * 64:half * 64 + cap, k, s * P:(s + 1) * P],
                                          giveT[half * 64:half * 64 + cap, k, c0:L], start=(k == 0), stop=(k == 1))
                        last.then_inc(p.spread, 1)

                def turn_gates(q, first):
                    pe.wait_ge(p.give_ready, q + 1)
                    if not first:
                        pe.wait_ge(p.added, 4 * q)
                    for k in range(2):
                        for t, o, n in reversed(tl):
                            last = tr(ps[:, 3 + 3 * k, o:o + n], give[0:n, k, t, :], ident[0:n, 0:n])
                        last.then_inc(p.give_turned, 1)

                def pair(i, q, first, last_):
                    if not last_:
                        pe.wait_ge(p.xg_ready, q + 1)
                        gather(i + 1)
                    if not first:
                        turn_hidden(2 * q - 1)
                    if last_ or first:
                        pe.wait_ge(p.xg_ready, q + 1)
                    up(q, 0)
                    if not first:
                        down(2 * q - 1, q - 1, 1)
                        spread(q - 1)
                    turn_gates(q, first)
                    turn_hidden(2 * q)
                    up(q, 1)
                    if not first:
                        pe.wait_ge(p.added, 4 * q)
                    down(2 * q, q, 0)

                q0 = done * PAIRS
                gather(0)
                pair(0, q0, True, False)
                with pe.Fori(1, PAIRS - 1) as i:
                    pair(i, q0 + i, False, False)
                qe = q0 + PAIRS - 1
                pair(PAIRS - 1, qe, False, True)
                turn_hidden(2 * qe + 1)
                down(2 * qe + 1, qe, 1)
                spread(qe)
                pe.wait_ge(p.added, 4 * qe + 4)

            def moe(l, rounds_before):
                router(l)
                pe.wait_ge(s_htok, htok_before[l] + 2 * len(tiles_of(l)))
                moe_round(first_path, l, l)
                pe.wait_ge(s_routed, l + 1)
                further = pe.value_load(extra[0:1, 0:1], min_val=0, max_val=MAX_ROUNDS - 1)
                with pe.If(further > 0):
                    with pe.Fori(0, further) as rr:
                        moe_round(further_path, l, pe.snap(rounds_before + rr))
                return further

            if stop == "mamba":
                return
            further = moe(0, 0)
            layer_norm(1)
            if stop == "moe0":
                return
            for j in range(2 * KD):
                w = unit(BASE_A, j // 4).rearrange("p (k f) -> p k f", k=KD)
                if j % 4 == 0:
                    pe.wait_ge(R_A.full[(BASE_A + j // 4) % RING], fills(0, j // 4))
                if j >= 4:
                    pe.wait_ge(a["kq_e"], j - 3)
                c0 = 0 if j < KD else META
                for k in range(KD):
                    if j == 0:
                        pe.wait_ge(s_ln, KD + k + 1)
                    last = mm(ps[:, j % 4, c0:L], w[:, k, (j % 4) * P:(j % 4 + 1) * P], hT[:, k, c0:L],
                              start=(k == 0), stop=(k == KD - 1))
                last.then_inc(a["kq"], 1)
            for half in range(2):
                w = unit(BASE_A, 4 + half).rearrange("p (k f) -> p k f", k=KD)
                pe.wait_ge(R_A.full[(BASE_A + 4 + half) % RING], fills(0, 4 + half))
                for t, (o, n) in enumerate(TILES):
                    v_ = 3 * half + t
                    if v_ >= 4:
                        pe.wait_ge(a["v_e"], v_ - 3)
                    for k in range(KD):
                        last = mm(ps[0:n, 4 + v_ % 4, :], hT[:, k, o:o + n], w[:, k, :],
                                  start=(k == 0), stop=(k == KD - 1))
                    last.then_inc(a["v"], 1)
            pe.wait_ge(a["kq_e"], 2 * KD)
            pe.wait_ge(a["v_e"], 6)
            pe.wait_ge(a["blocks"], 1)

            def scores(j):
                b = 3 * (j % 2)
                if j >= 2:
                    pe.wait_ge(a["w"], j - 1)
                for h in range(2):
                    r_ = slice(64 * h, 64 * h + 64)
                    mm(ps[:, b + h, 0:256], kT[r_, j, META:META + P], qT[r_, j, :],
                       start=True, stop=False, skip_group_check=True)
                for h in range(2):
                    r_ = slice(64 * h, 64 * h + 64)
                    mm(ps[:, b + h, 256:384], kT[r_, j, META + P:L], qT[r_, j, P:SEQ],
                       start=False, stop=False, skip_group_check=True)
                mm(ps[0:64, b + 2, 0:256], kz[:, j, :], qT[:, j, :],
                   start=True, stop=False, skip_group_check=True).then_inc(a["z"], 1)

            def log_weights(j):
                b, s_ = 3 * (j % 2), soft[:, j % 2, :]
                pe.wait_ge(a["sp"], j + 1)
                acc = dict(start=False, stop=False, skip_group_check=True)
                mm(ps[0:64, b + 2, 0:256], negfrom0[:, :], s_[0:64, 768:1024], **acc)
                for h in range(2):
                    s1, s2 = s_[:, 384 * h:384 * h + 256], s_[:, 384 * h + 256:384 * h + 384]
                    mm(ps[:, b + h, 0:256], negfrom[:, :], s1, **acc)
                    mm(ps[:, b + h, 128:256], negones[:, :], s2, **acc)
                    mm(ps[:, b + h, 256:384], negfrom[:, :], s2, **acc)
                    mm(ps[:, b + h, 0:128], ident[:, :], never[:, :], **acc)
                    mm(ps[:, b + h, 256:384], ident[:, :], never[:, :], **acc)
                    mm(ps[32 * h:32 * h + META, b + 2, 0:256], negones[:, 0:META], s1, **acc)
                    last = mm(ps[32 * h:32 * h + META, b + 2, 128:256], negones[:, 0:META], s2,
                              start=False, stop=True, skip_group_check=True)
                last.then_inc(a["arg"], 1)

            def values(j):
                w_ = wts[:, j % 2, :]
                o_ = ps[:, 6 + j % 2, :]
                pe.wait_ge(a["w"], j + 1)
                if j >= 2:
                    pe.wait_ge(a["o_e"], j - 1)
                if j == 0:
                    pe.wait_ge(a["vz"], 2)
                mm(o_[:, 0:256], vz[:, j, :], w_[0:64, 768:1024], start=True, stop=False, skip_group_check=True)
                for h in range(2):
                    r_ = slice(64 * h, 64 * h + 64)
                    f = slice(j * P + 64 * h, j * P + 64 * h + 64)
                    mm(o_[r_, 0:256], vtok[:, 1, f], w_[:, 384 * h:384 * h + 256],
                       start=False, stop=False, skip_group_check=True)
                    last = mm(o_[r_, 128:256], vtok[:, 2, f], w_[:, 384 * h + 256:384 * h + 384],
                              start=False, stop=True, skip_group_check=True)
                last.then_inc(a["o"], 1)

            scores(0)
            for j in range(KD):
                if j + 1 < KD:
                    scores(j + 1)
                log_weights(j)
                if j >= 1:
                    values(j - 1)
            values(KD - 1)
            pe.wait_ge(a["o_e"], KD)
            for mt in range(KD):
                w = unit(BASE_A, 6 + mt // 4).rearrange("p (k f) -> p k f", k=KD)
                if mt % 4 == 0:
                    pe.wait_ge(R_A.full[(BASE_A + 6 + mt // 4) % RING], fills(0, 6 + mt // 4))
                if mt >= 4:
                    pe.wait_ge(s_lnx, KD + mt - 3)
                for k in range(KD):
                    last = mm(ps[:, 4 + mt % 4, META:L], w[:, k, (mt % 4) * P:(mt % 4 + 1) * P], oT[:, k, :],
                              start=(k == 0), stop=(k == KD - 1))
                last.then_inc(a["outp"], 1)
                if mt > 0:
                    add_mean(2, mt - 1)
            layer_norm(2)
            if stop == "attn":
                return
            moe(1, further)
            layer_norm(3)
            n_ = 0
            for half in range(2):
                for t in (1, 2):
                    o, n = TILES[t]
                    for k in range(4):
                        pe.wait_ge(s_ln, 3 * KD + 4 * half + k + 1)
                        last = tr(ps[:, 2 + n_, k * P:(k + 1) * P], hT[:, 4 * half + k, o:o + n], ident[:, :])
                    last.then_inc(a["fin"], 1)
                    n_ += 1

        @block.scalar
        def _(act):
            sc = nc.scalar
            A = sc.activation
            link = Link(act, s_act)
            act.dma_start(prow[0:96, 0, :], mamba_conv_w[0].rearrange("w (c p) -> (w c) p", p=P)).then_inc(s_par, 16)
            act.dma_start(prow[96:120, 0, :], mamba_conv_b[0].rearrange("(c p) -> c p", p=P)).then_inc(s_par, 16)
            act.dma_start(dtb[:], mamba_dt_bias[0].rearrange("(e o) -> e o", o=1)).then_inc(s_ready0, 16)
            act.dma_start(alog[:], mamba_a_log[0].rearrange("(e o) -> e o", o=1)).then_inc(s_ready0, 16)
            for g6 in range(6):
                t, half = divmod(g6, 2)
                o, n = TILES[t]
                act.wait_ge(m["tin"], g6 + 1)
                A(hT[:, 4 * half:4 * half + 4, o:o + n],
                  ps[:, g6 % 4, :].rearrange("p (k n) -> p k n", k=4)[:, :, 0:n], ACT.Copy).then_inc(m["tin_e"], 1)
            act.wait_ge(s_ready0, 32)
            A(dtv[9][:, 0:1], alog[:, :], ACT.Exp).then_inc(m["dtea"], 1)
            act.wait_ge(m["dtn"], 1)
            A(dtv[2], dtv[1], ACT.Exp).then_inc(m["dtea"], 1)
            for c in range(CONV_TILES):
                if c == 13:
                    act.wait_ge(m["acp"], 1)
                    A(acT[:, :], ps[0:HEADS, 7, 0:L], ACT.Copy).then_inc(m["acs"], 1)
                act.wait_ge(m["conv_done"], c + 1)
                dst = bcT[:, c, :] if c < 8 else xsT[:, c - 8, :]
                A(dst, convw[:, c % 3, :], ACT.Silu).then_inc(m["xbc"], 1)
            for t, (o, n) in enumerate(TILES):
                A(dte[0:n, t, :], ps[0:n, 6, t * 32:t * 32 + 32], ACT.Exp).then_inc(m["dte_x"], 1)
            for t in range(2):
                n = TILES[t][1]
                act.wait_ge(m["bt"], t + 1)
                A(btok[0:n, t, :], ps[0:n, 4 + t, :], ACT.Copy).then_inc(m["btok"], 1)
            zt = 0

            def z_tile():
                nonlocal zt
                if zt < KI:
                    act.wait_ge(m["proj"], 1 + CONV_TILES + zt + 1)
                    if zt == 0:
                        act.wait_ge(m["da_r"], 3)
                    A(zT[:, zt, :], ps[:, 6 + zt % 2, 0:L], ACT.Copy).then_inc(m["z_read"], 1)
                    zt += 1

            for q in range(3 * GROUPS):
                t, grp = divmod(q, GROUPS)
                n = TILES[t][1]
                if t >= 1:
                    act.wait_ge(m["bc"], q + 1)
                    if q > GROUPS:
                        act.wait_ge(m["yps"], q)
                    A(cdec[:, 0:4, 0:n], ps[:, 2, :].rearrange("p (h l) -> p h l", h=4)[:, :, 0:n], ACT.Exp)
                    A(cdec[:, 4:8, 0:n], ps[:, 3, :].rearrange("p (h l) -> p h l", h=4)[:, :, 0:n], ACT.Exp)\
                        .then_inc(m["expc"], 1)
                act.wait_ge(m["dd"], q + 1)
                d = decay[0:n, q % 2, :, 0:n]
                A(d, d, ACT.Exp).then_inc(m["expd"], 1)
                z_tile()
                if q < 4:
                    z_tile()
            act.wait_ge(m["z_read"], KI)
            for grp in range(GROUPS):
                zg = zT[:, 4 * grp:4 * grp + 4, :]
                A(zg, zg, ACT.Silu).then_inc(m["zsilu"], 1)
            for grp in range(GROUPS):
                act.wait_ge(m["yz"], grp + 1)
                A(squares(grp), zT[:, 4 * grp:4 * grp + 4, :], ACT.Square).then_inc(m["rsq"], 1)
            sc.preload_act_table(ACT.Sqrt)
            for grp in range(GROUPS):
                act.wait_ge(m["rps"], grp + 1)
                A(rms(grp, 0), ps[:, grp, 0:L], ACT.Sqrt, bias=epsc[:, 0:1]).then_inc(m["rsd"], 1)

            def layer_norm(i):
                c0 = C0[i // 2]
                col = 16 + (i % 2) * 32 + (i // 2) * 8
                sc.preload_act_table(ACT.Sqrt)
                for quarter in range(4):
                    act.wait_ge(s_lnc, 4 * i + quarter + 1)
                    ks = slice(2 * quarter, 2 * quarter + 2)
                    A(sq[:, ks, c0:L], rT[:, ks, c0:L], ACT.Square).then_inc(s_lnq, 1)
                act.wait_ge(s_lnv, i + 1)
                A(stat[:, 0, c0:L], ps[:, 1, c0:L], ACT.Sqrt, bias=epsc[:, 0:1]).then_inc(s_lns, 1)
                for k in range(KD):
                    act.wait_ge(s_lnn, KD * i + k + 1)
                    A(hT[:, k, c0:L], rT[:, k, c0:L], ACT.Identity, scale=par2[:, col + k:col + k + 1],
                      bias=par2[:, col + 16 + k:col + 17 + k]).then_inc(s_ln, 1)

            layer_norm(0)

            def router(l):
                c0 = C0[l]
                act.wait_ge(s_router, l + 1)
                if l == 0:
                    act.wait_ge(s_rw, 32)
                A(logit[:, c0:L], ps[0:N_EXP, 2, c0:L], ACT.Identity, bias=rbias[:, 0:1]).then_inc(s_logit, 1)
                g_ = 0
                for t, o, n in tiles_of(l):
                    for half in range(2):
                        act.wait_ge(s_htok_ps, htok_before[l] + g_ + 1)
                        A(tok[0:n, t, 512 * half:512 * half + 512], ps[0:n, 4 + g_ % 2, :], ACT.Copy)\
                            .then_inc(s_htok, 1)
                        g_ += 1
                act.wait_ge(s_below, l + 1)
                A(route[:, 1, :], route[:, 1, :], ACT.Exp).then_inc(s_numer, 1)

            def moe_round(p, l, done):
                c0 = C0[l]

                def take_xg(q):
                    act.wait_ge(p.gathered, q + 1)
                    A(xg[:, 0:4, :], ps[:, 4, :].rearrange("p (k c) -> p k c", k=4)[:, :, 0:2 * cap], ACT.Copy)
                    A(xg[:, 4:8, :], ps[:, 5, :].rearrange("p (k c) -> p k c", k=4)[:, :, 0:2 * cap], ACT.Copy)\
                        .then_inc(p.xg_ready, 1)

                def take_hidT(x_):
                    act.wait_ge(p.hid_turned, x_ + 1)
                    A(hidT[:, :, :], ps[:, 1, 0:256].rearrange("p (a b) -> p a b", a=2), ACT.Copy)\
                        .then_inc(p.hidT_ready, 1)

                def silu(x_):
                    act.wait_ge(p.up_done, x_ + 1)
                    A(sg[:, :], ps[:, 0, 0:256], ACT.Silu).then_inc(p.silu_done, 1)

                def take_y(x_, k):
                    act.wait_ge(p.down_done, x_ + 1)
                    A(ysb[:, k, :], ps[:, 2, :], ACT.Copy).then_inc(p.y_ready, 1)

                def take_gates(q):
                    for k in range(2):
                        act.wait_ge(p.give_turned, 2 * q + k + 1)
                        A(giveT[:, k, c0:L], ps[:, 3 + 3 * k, c0:L], ACT.Copy).then_inc(p.giveT_ready, 1)

                def pair(q, first, last_):
                    if not first:
                        take_hidT(2 * q - 1)
                    silu(2 * q)
                    if not first:
                        take_y(2 * q - 1, 1)
                    take_gates(q)
                    take_hidT(2 * q)
                    silu(2 * q + 1)
                    if not last_:
                        take_xg(q + 1)
                    take_y(2 * q, 0)

                q0 = done * PAIRS
                take_xg(q0)
                pair(q0, True, False)
                with act.Fori(1, PAIRS - 1) as i:
                    pair(q0 + i, False, False)
                qe = q0 + PAIRS - 1
                pair(qe, False, True)
                take_hidT(2 * qe + 1)
                take_y(2 * qe + 1, 1)

            def moe(l, rounds_before):
                router(l)
                moe_round(first_path, l, l)
                act.wait_ge(s_routed, l + 1)
                further = act.value_load(extra[0:1, 0:1], min_val=0, max_val=MAX_ROUNDS - 1)
                with act.If(further > 0):
                    with act.Fori(0, further) as rr:
                        moe_round(further_path, l, act.snap(rounds_before + rr))
                return further

            if stop == "mamba":
                return
            further = moe(0, 0)
            layer_norm(1)
            if stop == "moe0":
                return
            for v_ in range(6):
                half, t = divmod(v_, 3)
                n = TILES[t][1]
                act.wait_ge(a["v"], v_ + 1)
                A(vtok[0:n, t, 512 * half:512 * half + 512], ps[0:n, 4 + v_ % 4, :], ACT.Copy).then_inc(a["v_e"], 1)
            act.wait_ge(a["v_e"], 6)
            act.wait_ge(a["blocks"], 1)
            v0 = vtok[0:META, 0, :].rearrange("p (j h d) -> p h j d", j=KD, h=2)
            for h in range(2):
                A(vz[32 * h:32 * h + META, :, 64 * h:64 * h + 64], v0[:, h], ACT.Copy).then_inc(a["vz"], 1)

            def soft_log(j):
                act.wait_ge(a["bound"], j + 1)
                parts = (soft[:, j % 2, 0:768], soft[0:64, j % 2, 768:1024])
                for v in parts:
                    A(v, v, ACT.Exp).then_inc(a["e"], 1)
                act.wait_ge(a["e"], 2 * j + 2)
                A(parts[0], parts[0], ACT.Ln, bias=1.0)
                A(parts[1], parts[1], ACT.Ln, bias=1.0).then_inc(a["ln"], 1)

            def weights(j):
                b = 3 * (j % 2)
                act.wait_ge(a["arg"], j + 1)
                if j >= 2:
                    act.wait_ge(a["o"], j - 1)
                A(wts[:, j % 2, 0:768].rearrange("p (h q) -> p h q", h=2), ps[:, b:b + 2, 0:384], ACT.Exp)
                A(wts[0:64, j % 2, 768:1024], ps[0:64, b + 2, 0:256], ACT.Exp).then_inc(a["w"], 1)

            sc.preload_act_table_set("natural_log_exp_and_others")
            soft_log(0)
            for j in range(KD):
                if j + 1 < KD:
                    soft_log(j + 1)
                weights(j)
            layer_norm(2)
            if stop == "attn":
                return
            moe(1, further)
            layer_norm(3)
            for n_ in range(4):
                half, t = n_ // 2, 1 + n_ % 2
                act.wait_ge(a["fin"], n_ + 1)
                A(tok[:, t, 512 * half:512 * half + 512], ps[:, 2 + n_, :], ACT.Copy).then_inc(a["fin_e"], 1)
                act.wait_ge(a["fin_e"], n_ + 1)
                act.dma_start(out[0, (t - 1) * P:t * P, 512 * half:512 * half + 512],
                              tok[:, t, 512 * half:512 * half + 512]).then_inc(a["store"], 16)
            act.wait_ge(a["store"], 64)

        @block.vector
        def _(dve):
            v = nc.vector
            link = Link(dve, s_dve)
            tt, ts, stt = v.tensor_tensor, v.tensor_scalar, v.scalar_tensor_tensor
            dve.wait_ge(m["ptr"], 1)
            v.tensor_copy(par1[:, :], ps[:, 4, 0:120]).then_inc(m["ptr_e"], 1)
            dve.wait_ge(m["ptr_e"], 1)
            dve.wait_ge(s_ready0, 32)
            dve.wait_ge(m["proj"], 1)
            ts(dtv[0], ps[0:HEADS, 0, 0:L], dtb[:, 0:1], None, ALU.add).then_inc(m["dtx"], 1)
            dve.wait_ge(m["dtx"], 1)
            stt(dtv[1], dtv[0], -1.0, dtv[0], ALU.mult, ALU.min).then_inc(m["dtn"], 1)

            def conv(c):
                ct = KI + c if c < 8 else c - 8
                src, dst = ps[:, 1 + c % 3, :], convw[:, c % 3, :]
                dve.wait_ge(m["proj"], c + 2)
                if c >= 3:
                    dve.wait_ge(m["xbc"], c - 2)
                tap = [par1[:, 24 * w + ct:24 * w + ct + 1] for w in range(CONV_W)]
                link(ts(dst, src[:, 0:L], tap[3], par1[:, 96 + ct:97 + ct], ALU.mult, ALU.add))
                for back in (1, 2, 3):
                    ins = stt(dst[:, back:L], src[:, 0:L - back], tap[3 - back], dst[:, back:L], ALU.mult, ALU.add)
                    if back < 3:
                        link(ins)
                    else:
                        ins.then_inc(m["conv_done"], 1)

            def dt_chain(part):
                x_, _, e_, d_, r_, s_, s2, p_, q_, ea = dtv
                if part == 0:
                    dve.wait_ge(m["dtea"], 2)
                    link(ts(d_, e_, 2.0, None, ALU.add))
                    link(v.reciprocal(r_, d_))
                if part == 1:
                    link(tt(s_, e_, r_, ALU.mult))
                    link(tt(s2, s_, s_, ALU.mult))
                    link(ts(p_, s2, 1.0 / 15, None, ALU.mult))
                if part in (2, 3):
                    for c_ in ((13, 11, 9), (7, 5, 3))[part - 2]:
                        link(stt(p_, p_, 1.0 / c_, s2, ALU.add, ALU.mult))
                if part == 4:
                    link(stt(q_, p_, 1.0, s_, ALU.add, ALU.mult))
                    link(ts(q_, q_, 2.0, None, ALU.mult))
                    link(stt(daT[0:HEADS], x_, 0.0, q_, ALU.max, ALU.add))
                    ts(daT[HEADS:2 * HEADS], daT[0:HEADS], ea[:, 0:1], -1.0, ALU.mult, ALU.mult)\
                        .then_inc(m["daT_r"], 1)

            for c in range(CONV_TILES):
                conv(c)
                if 1 <= c < 6:
                    dt_chain(c - 1)
                if c == 4:
                    dve.wait_ge(m["ptr"], 2)
                    v.tensor_copy(par2[:, :], ps[:, 4, 128:208]).then_inc(m["ptr_e"], 1)
                    dve.wait_ge(m["ptr_e"], 2)
                if c == 8:
                    dve.wait_ge(m["da_t"], 1)
                    for t, (o, n) in enumerate(TILES):
                        v.tensor_copy(da[0:n, t, :], ps[0:n, 5, t * 64:t * 64 + 64]).then_inc(m["da_r"], 1)
                if c == 11:
                    dve.wait_ge(m["acp"], 1)
                    for t, (o, n) in enumerate(TILES):
                        v.tensor_copy(acum[0:n, t, :], ps[0:n, 6, 96 + t * 32:128 + t * 32]).then_inc(m["acr"], 1)
            dve.wait_ge(m["acr"], 3)
            dve.wait_ge(m["xbc"], CONV_TILES)
            dve.wait_ge(s_skip, 32)

            def ssd_back(q):
                t, grp = divmod(q, GROUPS)
                o, n = TILES[t]
                dve.wait_ge(m["yps"], q + 1)
                for k in range(4):
                    j = grp * 4 + k
                    ins = stt(xsT[:, j, o:o + n], xsT[:, j, o:o + n], dskip[:, j:j + 1],
                              ps[:, 4, k * P:k * P + n], ALU.mult, ALU.add)
                ins.then_inc(m["yadd"], 1)
                if t < 2:
                    dve.wait_ge(m["stps"], q + 1)
                    if t == 0:
                        v.tensor_copy(state[:, grp * HPG:(grp + 1) * HPG, :],
                                      ps[:, 5, :].rearrange("p (h d) -> p h d", h=HPG)).then_inc(m["stup"], 1)
                    else:
                        dve.wait_ge(m["stup"], q)
                        for h in range(HPG):
                            s_ = state[:, grp * HPG + h, :]
                            ins = stt(s_, s_, lastd[:, q % 2, h:h + 1], ps[:, 5, h * HD:(h + 1) * HD],
                                      ALU.mult, ALU.add)
                        ins.then_inc(m["stup"], 1)

            for q in range(3 * GROUPS):
                t, grp = divmod(q, GROUPS)
                o, n = TILES[t]
                hs = slice(grp * HPG, (grp + 1) * HPG)
                dve.wait_ge(m["xtr"], q + 1)
                if q >= GROUPS:
                    dve.wait_ge(m["yps"], q - GROUPS + 1)
                    dve.wait_ge(m["xde"], q - GROUPS + 1)
                tt(xdt[0:n, hs, :], ps[0:n, 0, :].rearrange("p (h d) -> p h d", h=HPG),
                   da[0:n, t, hs].unsqueeze(2).broadcast_to([n, HPG, HD]), ALU.mult).then_inc(m["xdt"], 1)
                dve.wait_ge(m["cb"], q + 1)
                if q > 0:
                    dve.wait_ge(m["mt"], q)
                tt(cbm[0:n, 0:n], ps[0:n, 1, 0:n], upto[0:n, 0:n], ALU.mult).then_inc(m["cbm"], 1)
                dve.wait_ge(m["bc"], q + 1)
                if q >= 2:
                    dve.wait_ge(m["yps"], q - 1)
                if t >= 1:
                    dve.wait_ge(m["expc"], q - GROUPS + 1)
                for h in range(HPG):
                    hh = grp * HPG + h
                    ins = ts(decay[0:n, q % 2, h, 0:n], ps[0:n, 2 + h // 4, (h % 4) * P:(h % 4) * P + n],
                             acum[0:n, t, hh:hh + 1], 0.0, ALU.subtract, ALU.min)
                ins.then_inc(m["dd"], 1)
                if t >= 1:
                    if t == 1:
                        dve.wait_ge(m["stup"], q - 1)
                        link(v.tensor_copy(lastd[:, q % 2, :], cdec[:, :, n - 1]))
                    tt(cdec[:, :, 0:n], cdec[:, :, 0:n],
                       bcT[:, GROUPS + grp, o:o + n].unsqueeze(1).broadcast_to([P, HPG, n]),
                       ALU.mult).then_inc(m["cs"], 1)
                if q > 0:
                    ssd_back(q - 1)
            for grp in range(GROUPS):
                if grp == GROUPS - 1:
                    ssd_back(3 * GROUPS - 1)
                dve.wait_ge(m["yadd"], 2 * GROUPS + grp + 1)
                dve.wait_ge(m["zsilu"], grp + 1)
                g4 = slice(4 * grp, 4 * grp + 4)
                tt(zT[:, g4, :], zT[:, g4, :], xsT[:, g4, :], ALU.mult).then_inc(m["yz"], 1)
            for grp in range(GROUPS):
                dve.wait_ge(m["rsd"], grp + 1)
                link(v.reciprocal(rms(grp, 1), rms(grp, 0)))
                for k in range(4):
                    j = 4 * grp + k
                    stt(zT[:, j, :], zT[:, j, :], par2[:, j:j + 1], rms(grp, 1), ALU.mult, ALU.mult)\
                        .then_inc(m["yn"], 1)

            def residual(i, done):
                c0 = C0[i // 2]
                for mt in range(KD):
                    dve.wait_ge(done, mt + 1)
                    stt(rT[:, mt, c0:L], hT[:, mt, c0:L], ALPHA, ps[:, 4 + mt % 4, c0:L], ALU.mult, ALU.add)\
                        .then_inc(s_lnx, 1)

            def layer_norm(i):
                c0 = C0[i // 2]
                n = L - c0
                dve.wait_ge(s_lnm, i + 1)
                for quarter in range(4):
                    ks = slice(2 * quarter, 2 * quarter + 2)
                    tt(rT[:, ks, c0:L], rT[:, ks, c0:L], ps[:, 0, c0:L].unsqueeze(1).broadcast_to([P, 2, n]),
                       ALU.subtract).then_inc(s_lnc, 1)
                dve.wait_ge(s_lnc, 4 * i + 4)
                dve.wait_ge(s_lns, i + 1)
                link(v.reciprocal(stat[:, 1, c0:L], stat[:, 0, c0:L]))
                for k in range(KD):
                    tt(rT[:, k, c0:L], rT[:, k, c0:L], stat[:, 1, c0:L], ALU.mult).then_inc(s_lnn, 1)
                dve.wait_ge(s_ln, KD * (i + 1))

            residual(0, m["outp"])
            layer_norm(0)

            def place(x_, groups, out_, higher_first, buf):
                pi = x_.unsqueeze(2).broadcast_to([P, groups, 4, 4])
                pj = x_.unsqueeze(3).broadcast_to([P, groups, 4, 4])
                c0_, c1_ = (cmpb[:, n, 0:16 * groups].rearrange("p (g j i) -> p g j i", g=groups, j=4) for n in (0, 1))
                link(tt(c0_, pi, pj, ALU.is_gt))
                link(tt(c1_, pi, pj, ALU.is_ge))
                link(tt(c0_, c0_, higher[:, :, :].unsqueeze(1).broadcast_to([P, groups, 4, 4]), ALU.mult))
                link(tt(c1_, c1_, lower[:, :, :].unsqueeze(1).broadcast_to([P, groups, 4, 4]), ALU.mult))
                link(tt(c0_, c0_, c1_, ALU.add))
                link(v.tensor_reduce(out_, c0_, AX.X, ALU.add))

            def router(l):
                c0 = C0[l]
                link(v.memset(route[:, :, :], 0.0))
                link(v.memset(rank[:, :, :], -1.0))
                link(v.memset(gate[:, :, :], 0.0))
                link(ts(rT[:, :, c0:L], hT[:, :, c0:L], ALPHA, None, ALU.mult))
                t3 = [route[:, n, :].rearrange("p (t e) -> p t e", t=3) for n in range(12)]
                g12 = [route[:, n, :].rearrange("p (g j) -> p g j", j=PER_GRP) for n in range(12)]
                dve.wait_ge(s_turned, l + 1)
                for t, o, n in tiles_of(l):
                    link(v.tensor_copy(t3[0][0:n, t, :], ps[0:n, 3, t * N_EXP:(t + 1) * N_EXP]))
                top = route[:, 9, 0:3]
                link(v.tensor_reduce(top, t3[0], AX.X, ALU.max))
                tt(t3[1], t3[0], top.unsqueeze(2).broadcast_to([P, 3, N_EXP]), ALU.subtract).then_inc(s_below, 1)
                dve.wait_ge(s_numer, l + 1)
                total, inv = route[:, 9, 3:6], route[:, 9, 6:9]
                link(v.tensor_reduce(total, t3[1], AX.X, ALU.add))
                link(v.reciprocal(inv, total))
                link(tt(t3[2], t3[1], inv.unsqueeze(2).broadcast_to([P, 3, N_EXP]), ALU.mult))
                place(g12[2], 12, g12[3], None, 0)
                link(ts(t3[3], t3[3], 2.0, None, ALU.is_lt))
                link(tt(t3[4], t3[3], t3[2], ALU.mult))
                score, placed = route[:, 5, 0:12], route[:, 6, 0:12]
                link(v.tensor_reduce(score, g12[4], AX.X, ALU.add))
                place(score.rearrange("p (t g) -> p t g", t=3), 3, placed.rearrange("p (t g) -> p t g", t=3), None, 0)
                link(ts(placed, placed, 1.0, None, ALU.is_lt))
                tt(g12[8], g12[3], placed.unsqueeze(2).broadcast_to([P, 12, PER_GRP]), ALU.mult).then_inc(s_chosen, 1)
                dve.wait_ge(s_chosen, l + 1)
                link(tt(t3[7], t3[8], t3[2], ALU.mult))
                link(v.tensor_reduce(total, t3[7], AX.X, ALU.add))
                for t, o, n in tiles_of(l):
                    link(v.reciprocal(inv[0:n, t:t + 1], total[0:n, t:t + 1]))
                    link(ts(gate[0:n, t, 0:N_EXP], t3[7][0:n, t, :], inv[0:n, t:t + 1], None, ALU.mult))
                dve.wait_ge(s_counted, l + 1)
                for t, o, n in tiles_of(l):
                    link(stt(t3[10][0:n, t, :], ps[0:n, 2, t * N_EXP:(t + 1) * N_EXP], 1.0, t3[8][0:n, t, :],
                             ALU.add, ALU.mult))
                    link(ts(rank[0:n, t, 0:N_EXP], t3[10][0:n, t, :], -1.0, None, ALU.add))
                link(v.tensor_reduce(rmax[0:1, 0:1], ps[0:1, 2, 3 * N_EXP:4 * N_EXP], AX.X, ALU.max))
                link(ts(rmax[0:1, 1:2], rmax[0:1, 0:1], float(step), None, ALU.is_gt))
                for k in range(2, MAX_ROUNDS):
                    link(stt(rmax[0:1, 1:2], rmax[0:1, 0:1], float(step * k), rmax[0:1, 1:2], ALU.is_gt, ALU.add))
                v.tensor_copy(extra[0:1, 0:1], rmax[0:1, 1:2]).then_inc(s_routed, 1)
                dve.wait_ge(s_routed, l + 1)

            def moe_round(p, l, done, again):
                tl = tiles_of(l)
                c0 = C0[l]

                def make_pick(i):
                    for t, o, n in tl:
                        for k in range(2):
                            ins = ts(pick[0:n, t, k * cap:(k + 1) * cap], slots[0:n, :],
                                     rank[0:n, t, bass.ds(2 * i + k, 1)], None, ALU.is_equal)
                    ins.then_inc(p.pick_ready, 1)

                def make_give(i):
                    for k in range(2):
                        for t, o, n in tl:
                            ins = ts(give[0:n, k, t, :].rearrange("p (d c) -> p d c", d=2),
                                     slots[0:n, :].unsqueeze(1).broadcast_to([n, 2, cap]),
                                     rank[0:n, t, bass.ds(2 * i + k, 1)], gate[0:n, t, bass.ds(2 * i + k, 1)],
                                     ALU.is_equal, ALU.mult)
                    ins.then_inc(p.give_ready, 1)

                def make_hidden(x_):
                    dve.wait_ge(p.silu_done, x_ + 1)
                    tt(hid[:, :], sg[:, :], ps[:, 0, 256:512], ALU.mult).then_inc(p.hid_ready, 1)

                def add(q):
                    for s in range(4):
                        b0 = 6 if s % 2 == 0 else 2
                        dve.wait_ge(p.spread, 4 * q + s + 1)
                        r_ = rT[:, s:s + 5:4, c0:L]
                        tt(r_, r_, ps[:, b0:b0 + 2, c0:L], ALU.add).then_inc(p.added, 1)

                def pair(i, q, first, last_):
                    make_hidden(2 * q)
                    if not first:
                        add(q - 1)
                    if not last_:
                        dve.wait_ge(p.give_turned, 2 * q + 2)
                        make_give(i + 1)
                        dve.wait_ge(p.gathered, q + 2)
                        make_pick(i + 2)
                    make_hidden(2 * q + 1)

                if again:
                    ts(rank[:, :, :], rank[:, :, :], -float(step), None, ALU.add).then_inc(s_ranked, 1)
                    dve.wait_ge(s_ranked, done + 1)
                q0 = done * PAIRS
                make_pick(0)
                make_give(0)
                dve.wait_ge(p.gathered, q0 + 1)
                make_pick(1)
                pair(0, q0, True, False)
                with dve.Fori(1, PAIRS - 1) as i:
                    pair(i, q0 + i, False, False)
                qe = q0 + PAIRS - 1
                pair(PAIRS - 1, qe, False, True)
                add(qe)
                dve.wait_ge(p.added, 4 * qe + 4)

            def moe(l, rounds_before):
                router(l)
                moe_round(first_path, l, l, False)
                further = dve.value_load(extra[0:1, 0:1], min_val=0, max_val=MAX_ROUNDS - 1)
                with dve.If(further > 0):
                    with dve.Fori(0, further) as rr:
                        moe_round(further_path, l, dve.snap(rounds_before + rr), True)
                return further

            if stop == "mamba":
                return
            further = moe(0, 0)
            layer_norm(1)
            if stop == "moe0":
                return
            v.memset(kz, 0.0)
            v.memset(vz, 0.0).then_inc(a["blocks"], 1)
            dve.wait_ge(a["blocks"], 1)
            for j in range(2 * KD):
                dve.wait_ge(a["kq"], j + 1)
                if j < KD:
                    for h in range(2):
                        r_ = slice(64 * h, 64 * h + 64)
                        v.tensor_copy(kz[r_, j, 32 * h:32 * h + META], ps[r_, j % 4, 0:META])
                    v.tensor_copy(kT[:, j, :], ps[:, j % 4, 0:L]).then_inc(a["kq_e"], 1)
                else:
                    ts(qT[:, j - KD, :], ps[:, j % 4, META:L], HD ** -0.5, None, ALU.mult).then_inc(a["kq_e"], 1)

            def bound(j):
                b, s_ = 3 * (j % 2), soft[:, j % 2, :]
                dve.wait_ge(a["z"], j + 1)
                if j >= 2:
                    dve.wait_ge(a["arg"], j - 1)
                ts(s_[:, 0:768].rearrange("p (h q) -> p h q", h=2), ps[:, b:b + 2, 0:384], TOP, None, ALU.min)
                ts(s_[0:64, 768:1024], ps[0:64, b + 2, 0:256], TOP, None, ALU.min)\
                    .then_inc(a["bound"], 1)

            def softplus(j):
                b, s_ = 3 * (j % 2), soft[:, j % 2, :]
                dve.wait_ge(a["ln"], j + 1)
                s2 = s_[:, 0:768].rearrange("p (h q) -> p h q", h=2)
                tt(s2, ps[:, b:b + 2, 0:384], s2, ALU.max)
                link(tt(s_[0:64, 768:1024], ps[0:64, b + 2, 0:256], s_[0:64, 768:1024], ALU.max))
                mask = before[:, :].unsqueeze(1).broadcast_to([P, 2, P])
                tt(s2[:, :, 0:P], s2[:, :, 0:P], mask, ALU.mult)
                tt(s2[:, :, 256:384], s2[:, :, 256:384], mask, ALU.mult).then_inc(a["sp"], 1)

            def take_o(j):
                dve.wait_ge(a["o"], j + 1)
                v.tensor_copy(oT[:, j, :], ps[:, 6 + j % 2, 0:256]).then_inc(a["o_e"], 1)

            bound(0)
            for j in range(KD):
                if j + 1 < KD:
                    bound(j + 1)
                softplus(j)
                if j >= 1:
                    take_o(j - 1)
            take_o(KD - 1)
            residual(2, a["outp"])
            layer_norm(2)
            if stop == "attn":
                return
            moe(1, further)
            layer_norm(3)


_INS = ["x", "meta_tokens", "mamba_w_in", "mamba_conv_w", "mamba_conv_b", "mamba_dt_bias", "mamba_a_log",
        "mamba_d_skip", "mamba_norm_w", "mamba_w_out", "sb_w_q", "sb_w_o", "shared_w_k", "shared_w_v",
        "ln_mix_g", "ln_mix_b", "ln_ffn_g", "ln_ffn_b", "router_w", "router_b", "moe_w_gate", "moe_w_up",
        "moe_w_down"]


def kernel(**inputs):
    import numpy as _np
    import concourse.bacc as _bacc
    from concourse import mybir as _mybir
    from concourse.bass_utils import run_bass_kernel_spmd as _run

    nc = _bacc.Bacc("TRN2", target_bir_lowering=False, num_devices=1)
    arrays, args = {}, []
    for name in _INS:
        a = _np.ascontiguousarray(inputs[name])
        arrays[f"in_{name}_dram"] = a
        args.append(nc.dram_tensor(f"in_{name}_dram", a.shape, _mybir.dt.from_np(a.dtype), kind="ExternalInput").ap())
    args.append(nc.dram_tensor("out_dram", (1, SEQ, D_MODEL), _mybir.dt.float32, kind="ExternalOutput").ap())
    build_trunk(nc, *args)
    r = _run(nc, [arrays], core_ids=[0])
    return r.results[0]["out_dram"]
```

```python
from contextlib import ExitStack

import concourse.bass as bass
from concourse import mybir

F32 = mybir.dt.float32
F32R = mybir.dt.float32r
I32 = mybir.dt.int32
ALU = mybir.AluOpType
ACT = mybir.ActivationFunctionType
AX = mybir.AxisListType

P = 128
D_MODEL = 1024
KD = D_MODEL // P
META = 16
SEQ = 256
L = META + SEQ
TILES = [(0, META), (META, P), (META + P, P)]
DEPTH = 2
ALPHA = (2.0 * DEPTH) ** 0.25
EPS = 1e-5
TOP = 40.0
HEADS = 32
HD = 64
GROUPS = 4
HPG = HEADS // GROUPS
D_INNER = HEADS * HD
KI = D_INNER // P
CONV_TILES = KI + 2 * GROUPS
CONV_W = 4
SB_HEADS = 16
N_EXP = 16
N_GRP = 4
PER_GRP = N_EXP // N_GRP
D_EXP = 512
HALF = D_EXP // 2
CAP = 64
NEVER = 1e6
PAIRS = N_EXP // 2
PICKS = PAIRS + 1
UNIT = 4096
RING = 6
OUT_FROM = 2
SPLIT_FROM = 2
WARM = dict(route=6, ranks=6, norm=6)


class Link:

    def __init__(self, eng, sem):
        self.eng, self.sem, self.n = eng, sem, 0

    def __call__(self, ins):
        self.n += 1
        ins.then_inc(self.sem, 1)
        self.eng.wait_ge(self.sem, self.n)


def build_trunk(nc, x, meta_tokens, mamba_w_in, mamba_conv_w, mamba_conv_b, mamba_dt_bias,
                mamba_a_log, mamba_d_skip, mamba_norm_w, mamba_w_out, sb_w_q, sb_w_o,
                shared_w_k, shared_w_v, ln_mix_g, ln_mix_b, ln_ffn_g, ln_ffn_b,
                router_w, router_b, moe_w_gate, moe_w_up, moe_w_down, out, stop="", step=CAP):
    cap = CAP
    MAX_ROUNDS = -(-L // step)
    ctx = ExitStack()
    with ctx:
        def sb(name, shape, dt=F32):
            return ctx.enter_context(nc.sbuf_tensor(name, shape, dt))

        def sem(name):
            return ctx.enter_context(nc.semaphore(name))

        ps = ctx.enter_context(nc.psum_tensor("ps", [P, 8, 512], F32))
        ring = sb("ring", [P, RING, UNIT])
        hT = sb("hT", [P, KD, L])
        rT = sb("rT", [P, KD, L])
        tok = sb("tok", [P, 3, D_MODEL])
        ident = sb("ident", [P, P])
        upto = sb("upto", [P, P])
        after = sb("after", [P, P])
        before = sb("before", [P, P])
        negfrom = sb("negfrom", [P, P])
        ones = sb("ones", [P, P])
        negones = sb("negones", [P, P])
        negfrom0 = sb("negfrom0", [64, 64])
        never = sb("never", [P, P])
        mean_model = sb("mean_model", [P, P])
        mean_group = sb("mean_group", [P, P])
        slots = sb("slots", [P, cap])
        par1 = sb("par1", [P, 120])
        par2 = sb("par2", [P, 80])
        prow = sb("prow", [P, 2, P])
        dskip = sb("dskip", [P, KI])
        dtb = sb("dtb", [HEADS, 1])
        alog = sb("alog", [HEADS, 1])
        rbias = sb("rbias", [N_EXP, 1])
        epsc = sb("epsc", [P, 1])
        wdt = sb("wdt", [P, KD, HEADS])
        rw = sb("rw", [P, KD, N_EXP])
        logit = sb("logit", [N_EXP, L])
        route = sb("route", [P, 12, 3 * N_EXP])
        cmpb = sb("cmpb", [P, 3, 3 * N_EXP * PER_GRP])
        lower = sb("lower", [P, PER_GRP, PER_GRP])
        higher = sb("higher", [P, PER_GRP, PER_GRP])
        rank = sb("rank", [P, 3, N_EXP + 2])
        gate = sb("gate", [P, 3, N_EXP + 2])
        rmax = sb("rmax", [P, 4])
        extra = sb("extra", [1, 1], I32)
        PHASE = 15616
        with nc.sbuf_tensor("phase", [P, PHASE], F32) as phase:
            pass
        SPLIT = 2 * KD * L + 5 * KD * P
        split = sb("split", [P, PHASE], F32R)
        OUT_PARTS = 3 * KI * L
        split_more = sb("split_more", [P, 12, P], F32R)

        def carver():
            at = [0]

            def take(*shape, rows=P):
                n = 1
                for s in shape:
                    n *= s
                assert at[0] + n <= PHASE, at[0] + n
                v = phase[0:rows, at[0]:at[0] + n]
                at[0] += n
                if len(shape) == 2:
                    v = v.rearrange("p (a b) -> p a b", a=shape[0])
                if len(shape) == 3:
                    v = v.rearrange("p (a b c) -> p a b c", a=shape[0], b=shape[1])
                return v
            return take

        take = carver()
        zT = take(KI, L)
        xsT = take(KI, L)
        bcT = take(2 * GROUPS, L)
        xdt = take(HEADS, HD)
        state = take(HEADS, HD)
        convw = state.rearrange("p a b -> p (a b)")[:, 0:3 * L].rearrange("p (a b) -> p a b", a=3)
        tok_f = tok[:, :, :].rearrange("p a b -> p (a b)")
        decay = tok_f[:, 0:2048].rearrange("p (s h l) -> p s h l", s=2, h=HPG)
        xde = tok_f[:, 2048:2560].rearrange("p (h d) -> p h d", h=HPG)
        cbm = tok_f[:, 2560:2688]
        lastd = tok_f[:, 2688:2704].rearrange("p (s h) -> p s h", s=2)
        rT_f = rT[:, :, :].rearrange("p a b -> p (a b)")
        cdec = rT_f[:, 0:1024].rearrange("p (h l) -> p h l", h=HPG)
        btok = rT_f[:, 1024:2048].rearrange("p (t n) -> p t n", t=2)
        def squares(grp):
            return xsT[:, 4 * grp:4 * grp + 4, :]

        def rms(grp, inv):
            return bcT[:, GROUPS * inv + grp, :]

        y_high, y_low = (split[:, n * KI * L:(n + 1) * KI * L].rearrange("p (k n) -> p k n", k=KI) for n in (1, 2))
        wo_high = split[:, OUT_PARTS:OUT_PARTS + 2 * KD * P].rearrange("p (b k n) -> p b k n", b=2, k=KD)
        wo_rest = split[:, OUT_PARTS + 2 * KD * P:OUT_PARTS + 2 * KD * P + 4 * P].rearrange("p (k n) -> p k n", k=4)
        wo_low = ((split_more[:, 0:4, :], split_more[:, 4:8, :]), (split_more[:, 8:12, :], wo_rest))

        def out_weights(u):
            mt, half = OUT_FROM + u // 2, u % 2
            w = ring[:, (10 + mt // 2) % RING, :].rearrange("p (k f) -> p k f", k=KI)
            return 10 + mt // 2, w[:, half * KD:(half + 1) * KD, (mt % 2) * P:(mt % 2 + 1) * P]

        dtv = [zT[0:HEADS, n, :] for n in range(10)]
        daT = zT[0:2 * HEADS, 10, :]
        acT = tok[0:HEADS, :, :].rearrange("p a b -> p (a b)")[:, 2704:2704 + L]
        da = prow[:, :, :].rearrange("p a b -> p (a b)")[:, 0:192].rearrange("p (t h) -> p t h", t=3)
        dte = sb("dte", [P, 3, HEADS])
        acum = rT_f[:, 2048:2144].rearrange("p (t h) -> p t h", t=3)
        take = carver()
        sq = take(KD, L)
        xg = take(KD, 2 * cap)
        sg = take(2, HALF)
        hid = take(2, HALF)
        hidT = take(4, 2 * cap)
        ysb = take(D_MODEL)
        pick = take(3, 2 * cap)
        give = take(3, 2 * cap)
        giveT = take(L)
        stat = take(2, L)
        aside = take(2, UNIT)
        take = carver()
        oT = take(KD, SEQ)
        soft = take(2, 1024)
        wts = take(2, 1024)
        take(SPLIT - KD * SEQ - 4 * 1024)
        kT = take(KD, L)
        qT = take(KD, SEQ)
        kz = take(KD, 64)
        vz = take(KD, P, rows=64)
        vtok = tok
        h_high, h_low = (split[:, n * KD * L:(n + 1) * KD * L].rearrange("p (k n) -> p k n", k=KD) for n in (0, 1))
        w_parts = split[:, 2 * KD * L:SPLIT].rearrange("p (b k n) -> p b k n", b=5, k=KD)
        w_high, w_low = w_parts[:, 0:3], w_parts[:, 3:5]

        s_const = sem("s_const")
        s_xin = sem("s_xin")
        s_par = sem("s_par")
        s_par2 = sem("s_par2")
        s_wsm = sem("s_wsm")
        s_cstep = sem("s_cstep")
        s_dve = sem("s_dve")
        s_act = sem("s_act")
        s_ready0 = sem("s_ready0")
        s_skip = sem("s_skip")
        s_rw = sem("s_rw")

        class Ring:

            def __init__(self, name):
                self.full = [sem(f"{name}_full{s}") for s in range(RING)]

        def cols(w, lo, hi):
            return w[:, lo:hi].rearrange("(k p) f -> p k f", p=P)

        w_in, w_out = mamba_w_in[0], mamba_w_out[0]
        in_units = [8, 9, 4, 5, 6, 7, 0, 1, 2, 3]
        mamba_units = [cols(w_in, 512 * u, 512 * u + 512) for u in in_units] + \
                      [cols(w_out, 256 * u, 256 * u + 256) for u in range(4)]
        attn_units = [cols(w, 512 * u, 512 * u + 512)
                      for w in (shared_w_k, sb_w_q[0], shared_w_v, sb_w_o[0]) for u in range(2)]
        R_M, R_A = Ring("rm"), Ring("ra")
        BASE_M = 0
        BASE_A = 2

        def unit(base, n):
            return ring[:, (base + n) % RING, :]

        def fills(base, n):
            return 16 * (n // RING + 1)

        class Path:
            def __init__(self, tag):
                self.full = [sem(f"{tag}_full{s}") for s in range(3)]
                self.aside_full = sem(f"{tag}_aside_full")
                self.pick_ready = sem(f"{tag}_pick_ready")
                self.gathered = sem(f"{tag}_gathered")
                self.xg_ready = sem(f"{tag}_xg_ready")
                self.give_ready = sem(f"{tag}_give_ready")
                self.give_turned = sem(f"{tag}_give_turned")
                self.giveT_ready = sem(f"{tag}_giveT_ready")
                self.up_done = sem(f"{tag}_up_done")
                self.silu_done = sem(f"{tag}_silu_done")
                self.hid_ready = sem(f"{tag}_hid_ready")
                self.hid_turned = sem(f"{tag}_hid_turned")
                self.hidT_ready = sem(f"{tag}_hidT_ready")
                self.down_done = sem(f"{tag}_down_done")
                self.y_ready = sem(f"{tag}_y_ready")
                self.spread = sem(f"{tag}_spread")
                self.added = sem(f"{tag}_added")

        first_path, further_path = Path("first"), Path("further")
        FILL = 64
        SLOT_BASE = [1, 2]

        def slot_unit(layer, slot, e):
            return 2 * ((SLOT_BASE[layer] + slot) % 3) + e
        s_ranked = sem("s_ranked")
        s_router = sem("s_router")
        s_logit = sem("s_logit")
        s_turned = sem("s_turned")
        s_below = sem("s_below")
        s_numer = sem("s_numer")
        s_chosen = sem("s_chosen")
        s_counted = sem("s_counted")
        s_routed = sem("s_routed")
        s_htok_ps = sem("s_htok_ps")
        s_htok = sem("s_htok")
        htok_before = [0, 6]
        s_lnx = sem("s_lnx")
        s_lnm = sem("s_lnm")
        s_lnc = sem("s_lnc")
        s_lnq = sem("s_lnq")
        s_lnv = sem("s_lnv")
        s_lns = sem("s_lns")
        s_lnn = sem("s_lnn")
        s_ln = sem("s_ln")
        names = ("tin", "tin_e", "ptr", "ptr_e", "acr", "proj", "conv_done", "xbc", "z_read", "dtx", "dtn", "dte_e",
                 "dtea", "da_t", "daT_r", "da_r", "acp", "acs", "dte_x", "bt", "btok", "xtr", "xdt", "bc",
                 "cb", "cbm", "dd", "expd", "expc", "mt", "cs", "yps", "yadd", "xde", "stps", "stup",
                 "zsilu", "yz", "rsq", "rps", "rsd", "yn", "yhi", "ylo", "whi", "wlo", "half", "outp", "outr")
        m = {n: sem(f"m_{n}") for n in names}
        anames = ("kq", "kq_e", "hhi", "hlo", "whi", "wlo", "v", "v0", "v_e", "blocks", "vz", "z", "bound", "e", "ln", "sp", "arg", "w", "o", "o_e",
                  "outp", "outr", "fin", "fin_e", "store")
        a = {n: sem(f"a_{n}") for n in anames}

        rnd_tokens = [TILES, TILES[1:]]
        C0 = [0, META]

        def tiles_of(layer):
            return [(t, o, n) for t, (o, n) in enumerate(TILES) if t >= layer]

        block = ctx.enter_context(nc.Block())

        @block.gpsimd
        def _(pool):
            g = nc.gpsimd
            for n, (t, v) in enumerate(((ident, 1.0), (upto, 1.0), (after, 1.0), (before, 1.0),
                                        (negfrom, -1.0), (lower, 1.0), (higher, 1.0), (never, -1e30))):
                g.memset(t[:], v).then_inc(s_cstep, 1)
            g.memset(negfrom0[:], 0.0).then_inc(s_cstep, 1)
            g.memset(epsc[:], EPS).then_inc(s_cstep, 1)
            g.memset(ones[:], 1.0).then_inc(s_cstep, 1)
            g.memset(negones[:], -1.0).then_inc(s_cstep, 1)
            g.memset(mean_model[:], 1.0 / D_MODEL).then_inc(s_cstep, 1)
            g.memset(mean_group[:], 1.0 * GROUPS / D_INNER).then_inc(s_cstep, 1)
            pool.wait_ge(s_cstep, 14)

            def select(t, op, cm, pattern):
                g.affine_select(out=t, in_=t, compare_op=op, fill=0.0, base=0, pattern=pattern,
                                channel_multiplier=cm).then_inc(s_const, 1)

            select(ident[:], ALU.is_equal, 1, [[-1, P]])
            select(upto[:], ALU.is_ge, -1, [[1, P]])
            select(after[:], ALU.is_gt, 1, [[-1, P]])
            select(before[:], ALU.is_gt, -1, [[1, P]])
            select(negfrom[:], ALU.is_ge, 1, [[-1, P]])
            select(lower[:], ALU.is_gt, 0, [[1, PER_GRP], [-1, PER_GRP]])
            select(higher[:], ALU.is_gt, 0, [[-1, PER_GRP], [1, PER_GRP]])
            select(never[:], ALU.is_ge, 1, [[-1, P]])
            g.iota(slots[:], [[1, cap]], base=0, channel_multiplier=0,
                   allow_small_or_imprecise_dtypes=True).then_inc(s_const, 1)
            pool.wait_ge(s_const, 9)
            g.tensor_copy(negfrom0[0:META, 0:META], negfrom[0:META, 0:META])
            if step < cap:
                g.memset(slots[:, step:cap], NEVER).then_inc(s_cstep, 1)
                pool.wait_ge(s_cstep, 15)
            g.tensor_copy(negfrom0[32:32 + META, 32:32 + META], negfrom[0:META, 0:META]).then_inc(s_const, 1)
            for q in range(3 * GROUPS):
                t, grp = divmod(q, GROUPS)
                n = TILES[t][1]
                if t < 2:
                    pool.wait_ge(m["xdt"], q + 1)
                    if q == 0:
                        pool.wait_ge(m["dte_x"], 3)
                    else:
                        pool.wait_ge(m["stps"], q)
                    g.tensor_tensor(xde[0:n], xdt[0:n, grp * HPG:(grp + 1) * HPG, :],
                                    dte[0:n, t, grp * HPG:(grp + 1) * HPG].unsqueeze(2).broadcast_to([n, HPG, HD]),
                                    ALU.mult).then_inc(m["xde"], 1)
                pool.wait_ge(m["cbm"], q + 1)
                pool.wait_ge(m["expd"], q + 1)
                d = decay[0:n, q % 2, :, 0:n]
                g.tensor_tensor(d, d, cbm[0:n, 0:n].unsqueeze(1).broadcast_to([n, HPG, n]),
                                ALU.mult).then_inc(m["mt"], 1)

        @block.sync
        def _(sp):
            def send(sem_, base, n, src):
                dst = unit(base, n)
                if len(src.shape) == 3:
                    dst = dst.rearrange("p (a b) -> p a b", a=src.shape[1])
                sp.dma_start(dst, src).then_inc(sem_, 16)

            sp.dma_start(tok[0:META, 0, :], meta_tokens).then_inc(s_xin, 16)
            for t in (1, 2):
                sp.dma_start(tok[:, t, :], x[0, (t - 1) * P:t * P, :]).then_inc(s_xin, 16)
            sp.dma_start(wdt[:], cols(w_in, 5120, 5152)).then_inc(s_wsm, 16)
            for n, src in enumerate(mamba_units):
                if n == 1:
                    sp.dma_start(prow[0:16, 1, :], mamba_norm_w[0].rearrange("(c p) -> c p", p=P))\
                        .then_inc(s_par2, 16)
                    for r, v in enumerate((ln_mix_g, ln_mix_b, ln_ffn_g, ln_ffn_b)):
                        sp.dma_start(prow[16 + 16 * r:32 + 16 * r, 1, :], v.rearrange("l (c p) -> (l c) p", p=P))\
                            .then_inc(s_par2, 16)
                    sp.wait_ge(s_par, 32)
                    sp.wait_ge(s_ready0, 32)
                if n == 3:
                    dsk = mamba_d_skip.rearrange("o (t two) -> o two t", two=2)
                    for par in range(2):
                        sp.dma_start(dskip[par * 64:par * 64 + 64, :], dsk[:, par, :].broadcast_to([64, KI]),
                                     allow_slow_non_contiguous=True).then_inc(s_skip, 16)
                    sp.dma_start(rbias[:], router_b.rearrange("(e o) -> e o", o=1)).then_inc(s_rw, 16)
                    sp.dma_start(rw[:], router_w.rearrange("(k p) e -> p k e", p=P)).then_inc(s_rw, 16)
                if n >= RING:
                    sp.wait_ge(m["proj"], 1 + 4 * (n - RING + 1))
                if n >= 10:
                    dst = unit(BASE_M, n).rearrange("p (a b) -> p a b", a=KI)
                    sp.dma_start(dst, src).then_inc(R_M.full[(BASE_M + n) % RING], 16)
                else:
                    send(R_M.full[(BASE_M + n) % RING], BASE_M, n, src)

            def send_half(p, layer, slot, i, half, before=(None, None)):
                for e in range(2):
                    if before[e]:
                        sp.wait_ge(*before[e])
                    dst = ring[:, slot_unit(layer, slot, e), :].rearrange("p (k g f) -> p k g f", k=KD, g=2)
                    for g_, w in enumerate((moe_w_gate[layer], moe_w_up[layer])):
                        src = w[bass.ds(2 * i + e, 1), :, half * HALF:(half + 1) * HALF]\
                            .rearrange("o (k p) f -> p (o k) f", p=P)
                        sp.dma_start(dst[:, :, g_, :], src).then_inc(p.full[slot], 16)

            def send_down(p, layer, slot, i):
                for e in range(2):
                    at, sem_ = (aside[:, e, :], p.aside_full) if slot is None else \
                               (ring[:, slot_unit(layer, slot, e), :], p.full[slot])
                    dst = at.rearrange("p (b d) -> p b d", b=4)
                    for b2 in range(2):
                        src = moe_w_down[layer][bass.ds(2 * i + e, 1), b2 * HALF:(b2 + 1) * HALF, :]\
                            .rearrange("o (b p) d -> p (o b) d", p=P)
                        sp.dma_start(dst[:, 2 * b2:2 * b2 + 2, :], src).then_inc(sem_, 16)

            def moe_round(p, layer, q0, before):
                send_half(p, layer, 0, 0, 0, before[0:2])
                send_half(p, layer, 1, 0, 1, before[2:4])
                send_half(p, layer, 2, 1, 0, before[4:6])
                if before[6]:
                    sp.wait_ge(*before[6])
                send_down(p, layer, None, 0)
                sp.wait_ge(p.up_done, 2 * q0 + 1)
                send_down(p, layer, 0, 1)
                sp.wait_ge(p.up_done, 2 * q0 + 2)
                send_half(p, layer, 1, 1, 1)
                sp.wait_ge(p.up_done, 2 * q0 + 3)
                send_half(p, layer, 2, 2, 0)
                sp.wait_ge(p.up_done, 2 * q0 + 4)
                send_half(p, layer, 1, 2, 1)
                with sp.Fori(3, PAIRS) as i:
                    q = q0 + i
                    sp.wait_ge(p.up_done, 2 * q - 1)
                    send_half(p, layer, 2, i, 0)
                    sp.wait_ge(p.down_done, q - 1)
                    send_down(p, layer, 0, i - 1)
                    sp.wait_ge(p.up_done, 2 * q)
                    send_half(p, layer, 1, i, 1)
                sp.wait_ge(p.up_done, 2 * (q0 + PAIRS) - 1)
                send_down(p, layer, 2, PAIRS - 1)

            def moe_stream(layer, before, rounds_before):
                moe_round(first_path, layer, layer * PAIRS, before)
                sp.wait_ge(s_routed, layer + 1)
                further = sp.value_load(extra[0:1, 0:1], min_val=0, max_val=MAX_ROUNDS - 1)
                with sp.If(further > 0):
                    with sp.Fori(0, further) as rr:
                        done = sp.snap(rounds_before + rr)
                        sp.wait_ge(s_ranked, done + 1)
                        moe_round(further_path, layer, done * PAIRS, (None,) * 7)
                    sp.wait_ge(s_lnm, 2 * layer + 2)
                return further

            if stop == "mamba":
                return
            op = m["outp"]
            further = moe_stream(0, ((m["proj"], 37), (m["proj"], 41), (op, 2), (op, 4), (op, 6), (op, 8), (op, 8)), 0)
            if stop == "moe0":
                return
            pf = first_path
            free = [(pf.down_done, PAIRS - 1)] * 2 + [(pf.up_done, 2 * PAIRS)] * 2 + \
                   [(pf.down_done, PAIRS)] * 2 + [(a["kq"], 4), (a["kq"], 8)]
            for n, src in enumerate(attn_units):
                sp.wait_ge(*free[n])
                send(R_A.full[(BASE_A + n) % RING], BASE_A, n, src)
            if stop == "attn":
                return
            moe_stream(1, ((a["kq"], 12), (a["kq"], 16), (a["v0"], 1), (a["v0"], 2), (a["outp"], 4), (a["outp"], 8),
                           (a["o_e"], KD)),
                       further)

        @block.tensor
        def _(pe):
            mm = nc.tensor.matmul
            tr = nc.tensor.transpose
            pe.wait_ge(s_const, 10)
            pe.wait_ge(s_xin, 48)
            for g6 in range(6):
                t, half = divmod(g6, 2)
                n = TILES[t][1]
                if g6 >= 4:
                    pe.wait_ge(m["tin_e"], g6 - 3)
                for k in range(4):
                    kk = 4 * half + k
                    last = tr(ps[:, g6 % 4, k * P:k * P + n], tok[0:n, t, kk * P:(kk + 1) * P], ident[0:n, 0:n])
                last.then_inc(m["tin"], 1)
            pe.wait_ge(s_par, 32)
            tr(ps[:, 4, 0:120], prow[0:120, 0, :], ident[0:120, 0:120]).then_inc(m["ptr"], 1)
            pe.wait_ge(m["tin_e"], 6)
            pe.wait_ge(s_wsm, 16)
            for k in range(KD):
                last = mm(ps[0:HEADS, 0, 0:L], wdt[:, k, :], hT[:, k, :], start=(k == 0), stop=(k == KD - 1))
            last.then_inc(m["proj"], 1)

            def project(n_unit, j, bank):
                w = unit(BASE_M, n_unit).rearrange("p (k f) -> p k f", k=KD)
                if j == 0:
                    pe.wait_ge(R_M.full[(BASE_M + n_unit) % RING], fills(BASE_M, n_unit))
                for k in range(KD):
                    last = mm(ps[:, bank, 0:L], w[:, k, j * P:(j + 1) * P], hT[:, k, :],
                              start=(k == 0), stop=(k == KD - 1))
                last.then_inc(m["proj"], 1)
                return last

            def stay_warm(n):
                for _ in range(n):
                    mm(ps[:, 7, 0:256], ident[:, :],
                       ident[:, :].unsqueeze(1).broadcast_to([P, 2, P]), start=True, stop=True)

            def add_mean(i, k):
                c0 = C0[i // 2]
                if i % 2 == 0:
                    pe.wait_ge(s_lnx, KD * (i // 2) + k + 1)
                ins = mm(ps[:, 0, c0:L], mean_model[:, :], rT[:, k, c0:L], start=(k == 0), stop=(k >= KD - 2),
                         skip_group_check=True)
                if k == KD - 1:
                    ins.then_inc(s_lnm, 1)

            def layer_norm(i):
                c0 = C0[i // 2]
                add_mean(i, KD - 1)
                for k in range(KD):
                    if k % 2 == 0:
                        pe.wait_ge(s_lnq, 4 * i + k // 2 + 1)
                    last = mm(ps[:, 1, c0:L], mean_model[:, :], sq[:, k, c0:L], start=(k == 0), stop=(k == KD - 1))
                last.then_inc(s_lnv, 1)
                stay_warm(WARM["norm"])

            for c in range(CONV_TILES):
                if c >= 3:
                    pe.wait_ge(m["conv_done"], c - 2)
                project(c // 4, c % 4, 1 + c % 3)
                if c == 4:
                    pe.wait_ge(s_par2, 16 * 5)
                    pe.wait_ge(m["ptr_e"], 1)
                    tr(ps[:, 4, 128:208], prow[0:80, 1, :], ident[0:80, 0:80]).then_inc(m["ptr"], 1)
                if c == 6:
                    pe.wait_ge(m["daT_r"], 1)
                    for t, (o, n) in enumerate(TILES):
                        last = tr(ps[0:n, 5, t * 64:t * 64 + 64], daT[:, o:o + n], ident[0:64, 0:64])
                    last.then_inc(m["da_t"], 1)
                if c == 10:
                    pe.wait_ge(m["da_r"], 3)
                    for t, (o, n) in enumerate(TILES):
                        a_t = da[0:n, t, HEADS:2 * HEADS]
                        mm(ps[0:n, 6, t * 32:t * 32 + 32], after[0:n, 0:n], a_t, start=True, stop=True)
                        mm(ps[0:n, 6, 96 + t * 32:128 + t * 32], upto[0:n, 0:n], a_t, start=True, stop=True)
                        last = mm(ps[0:HEADS, 7, o:o + n], a_t, upto[0:n, 0:n], start=True, stop=True)
                    last.then_inc(m["acp"], 1)
                if c == 12:
                    pe.wait_ge(m["xbc"], GROUPS)
                    pe.wait_ge(m["ptr_e"], 2)
                    for t in range(2):
                        o, n = TILES[t]
                        for grp in range(GROUPS):
                            last = tr(ps[0:n, 4 + t, grp * P:(grp + 1) * P], bcT[:, grp, o:o + n], ident[:, :])
                        last.then_inc(m["bt"], 1)

            def ssd_front(q):
                t, grp = divmod(q, GROUPS)
                o, n = TILES[t]
                if q == 0:
                    pe.wait_ge(m["dtx"], 1)
                else:
                    pe.wait_ge(m["xdt"], q)
                for k in range(4):
                    last = tr(ps[0:n, 0, k * P:(k + 1) * P], xsT[:, grp * 4 + k, o:o + n], ident[:, :])
                last.then_inc(m["xtr"], 1)
                if q == 0:
                    pe.wait_ge(m["acs"], 1)
                else:
                    pe.wait_ge(m["dd"], q)
                    if q > GROUPS:
                        pe.wait_ge(m["expc"], q - GROUPS)
                for h in range(HPG):
                    hh = grp * HPG + h
                    last = mm(ps[:, 2 + h // 4, (h % 4) * P:(h % 4) * P + n],
                              ident[0:HEADS, hh:hh + 1].broadcast_to([HEADS, P]), acT[:, o:o + n],
                              start=True, stop=True)
                last.then_inc(m["bc"], 1)
                if q > 0:
                    pe.wait_ge(m["cbm"], q)
                mm(ps[0:n, 1, 0:n], bcT[:, grp, o:o + n], bcT[:, GROUPS + grp, o:o + n],
                   start=True, stop=True).then_inc(m["cb"], 1)

            def ssd_back(q):
                t, grp = divmod(q, GROUPS)
                o, n = TILES[t]
                pe.wait_ge(m["mt"], q + 1)
                if t >= 1:
                    pe.wait_ge(m["cs"], q - GROUPS + 1)
                    pe.wait_ge(m["stup"], min(q - GROUPS + 1, 2 * GROUPS))
                if q > 0:
                    pe.wait_ge(m["yadd"], q)
                for h in range(HPG):
                    hh = grp * HPG + h
                    dst = ps[(h % 2) * HD:(h % 2) * HD + HD, 4, (h // 2) * P:(h // 2) * P + n]
                    last = mm(dst, xdt[0:n, hh, :], decay[0:n, q % 2, h, 0:n], start=True, stop=(t == 0))
                    if t >= 1:
                        last = mm(dst, state[:, hh, :], cdec[:, h, 0:n], start=False, stop=True)
                last.then_inc(m["yps"], 1)
                if t < 2:
                    pe.wait_ge(m["xde"], q + 1)
                    if q > 0:
                        pe.wait_ge(m["stup"], q)
                    if q == 0:
                        pe.wait_ge(m["btok"], 2)
                    mm(ps[:, 5, :], btok[0:n, t, grp * P:(grp + 1) * P], xde[0:n].rearrange("p h d -> p (h d)"),
                       start=True, stop=True).then_inc(m["stps"], 1)

            zt = 0

            def z_tile():
                nonlocal zt
                if zt < KI:
                    if zt == 0:
                        pe.wait_ge(m["dte_x"], 3)
                        pe.wait_ge(m["acr"], 3)
                    if zt >= 2:
                        pe.wait_ge(m["z_read"], zt - 1)
                    project(6 + zt // 4, zt % 4, 6 + zt % 2)
                    zt += 1

            z_tile()
            pe.wait_ge(m["acs"], 1)
            pe.wait_ge(m["xbc"], CONV_TILES)
            for q in range(3 * GROUPS):
                if q == 0:
                    pe.wait_ge(m["btok"], 2)
                ssd_front(q)
                if q < 3:
                    z_tile()
                if q > 0:
                    ssd_back(q - 1)
                z_tile()
            ssd_back(3 * GROUPS - 1)
            for grp in range(GROUPS):
                pe.wait_ge(m["rsq"], grp + 1)
                if grp == 0:
                    pe.wait_ge(m["xdt"], 3 * GROUPS)
                    pe.wait_ge(m["dd"], 3 * GROUPS)
                    pe.wait_ge(m["cbm"], 3 * GROUPS)
                    pe.wait_ge(m["expc"], 2 * GROUPS)
                for k in range(4):
                    last = mm(ps[:, grp, 0:L], mean_group[:, :], squares(grp)[:, k, :], start=(k == 0), stop=(k == 3))
                last.then_inc(m["rps"], 1)
            pe.wait_ge(m["z_read"], KI)
            pe.wait_ge(m["yadd"], 3 * GROUPS)
            pe.wait_ge(m["stup"], 2 * GROUPS)
            w = unit(BASE_M, 10).rearrange("p (k f) -> p k f", k=KI)
            pe.wait_ge(R_M.full[(BASE_M + 10) % RING], fills(BASE_M, 10))
            for k in range(KI):
                pe.wait_ge(m["yn"], k + 1)
                for mt in range(2):
                    ins = mm(ps[:, 4 + mt, 0:L], w[:, k, mt * P:(mt + 1) * P], zT[:, k, :],
                             start=(k == 0), stop=(k == KI - 1))
                    if k == KI - 1:
                        ins.then_inc(m["outp"], 1)
            for mt in range(2, KD):
                if mt >= 4:
                    pe.wait_ge(s_lnx, mt - 3)
                for half in range(2):
                    u = 2 * (mt - OUT_FROM) + half
                    pe.wait_ge(m["wlo"], u + 1)
                    if u == 0:
                        pe.wait_ge(m["ylo"], GROUPS)
                    for kk in range(KD):
                        k = half * KD + kk
                        w_hi, w_lo = wo_high[:, u % 2, kk, :], wo_low[u % 2][kk // 4][:, kk % 4, :]
                        dst = ps[:, 4 + mt % 4, 0:L]
                        mm(dst, w_hi, y_low[:, k, :], start=(k == 0), stop=False)
                        mm(dst, w_lo, y_high[:, k, :], start=False, stop=False)
                        last = mm(dst, w_hi, y_high[:, k, :], start=False, stop=(k == KI - 1))
                    if half == 0:
                        last.then_inc(m["half"], 1)
                last.then_inc(m["outp"], 1)
                for k in range(0 if mt == 2 else mt - 1, mt):
                    add_mean(0, k)

            layer_norm(0)

            def router(l):
                c0 = C0[l]
                i = 2 * l
                if l == 0:
                    pe.wait_ge(s_rw, 32)
                for k in range(KD):
                    pe.wait_ge(s_ln, KD * i + k + 1)
                    last = mm(ps[0:N_EXP, 2, c0:L], rw[:, k, :], hT[:, k, c0:L], start=(k == 0), stop=(k == KD - 1))
                last.then_inc(s_router, 1)
                pe.wait_ge(s_logit, l + 1)
                for t, o, n in tiles_of(l):
                    last = tr(ps[0:n, 3, t * N_EXP:(t + 1) * N_EXP], logit[:, o:o + n], ident[0:N_EXP, 0:N_EXP])
                last.then_inc(s_turned, 1)
                g_ = 0
                for t, o, n in tiles_of(l):
                    for half in range(2):
                        if g_ >= 2:
                            pe.wait_ge(s_htok, htok_before[l] + g_ - 1)
                        for k in range(4):
                            last = tr(ps[0:n, 4 + g_ % 2, k * P:(k + 1) * P],
                                      hT[:, 4 * half + k, o:o + n], ident[:, :])
                        last.then_inc(s_htok_ps, 1)
                        g_ += 1
                stay_warm(WARM["route"])
                pe.wait_ge(s_chosen, l + 1)
                sel = route[:, 8, :].rearrange("p (t e) -> p t e", t=3)
                tl = tiles_of(l)
                for t, o, n in tl:
                    for t2, o2, n2 in tl:
                        if t2 <= t:
                            lhs = before[0:n, 0:n] if t2 == t else ones[0:n2, 0:n]
                            mm(ps[0:n, 2, t * N_EXP:(t + 1) * N_EXP], lhs, sel[0:n2, t2, :],
                               start=(t2 == tl[0][0]), stop=(t2 == t))
                for t, o, n in tl:
                    last = mm(ps[:, 2, 3 * N_EXP:4 * N_EXP], ones[0:n, :], sel[0:n, t, :],
                              start=(t == tl[0][0]), stop=(t == 2))
                last.then_inc(s_counted, 1)
                stay_warm(WARM["ranks"])

            def moe_round(p, l, done):
                tl = tiles_of(l)
                c0 = C0[l]

                def gather(i_next):
                    pe.wait_ge(p.pick_ready, done * PICKS + i_next + 1)
                    for k in range(KD):
                        for t, o, n in tl:
                            last = mm(ps[:, 6 + k // 4, (k % 4) * P:(k % 4) * P + 2 * cap],
                                      tok[0:n, t, k * P:(k + 1) * P], pick[0:n, t, :],
                                      start=(t == tl[0][0]), stop=(t == 2))
                    last.then_inc(p.gathered, 1)

                def up(slot, fill, half):
                    pe.wait_ge(p.full[slot], FILL * fill)
                    for kk in range(KD):
                        for e in range(2):
                            w = ring[:, slot_unit(l, slot, e), :].rearrange("p (k f) -> p k f", k=KD)
                            last = mm(ps[e * 64:e * 64 + cap, half, :], xg[:, kk, e * cap:(e + 1) * cap],
                                      w[:, kk, :], start=(kk == 0), stop=(kk == KD - 1))
                    last.then_inc(p.up_done, 1)

                def turn_hidden(q, half):
                    pe.wait_ge(p.hid_ready, 2 * q + half + 1)
                    for j in range(2):
                        last = tr(ps[:, 2, j * P:(j + 1) * P], hid[:, half, j * P:(j + 1) * P], ident[:, :])
                    last.then_inc(p.hid_turned, 1)

                def turn_gates(q):
                    pe.wait_ge(p.give_ready, q + 1)
                    for t, o, n in reversed(tl):
                        last = tr(ps[:, 3, o:o + n], give[0:n, t, :], ident[0:n, 0:n])
                    last.then_inc(p.give_turned, 1)

                def down(q, slot, fill):
                    pe.wait_ge(p.hidT_ready, 2 * q + 2)
                    pe.wait_ge(p.aside_full if slot is None else p.full[slot], FILL * fill)
                    for b in range(4):
                        for dh in range(2):
                            for e in range(2):
                                at = aside[:, e, :] if slot is None else ring[:, slot_unit(l, slot, e), :]
                                w = at.rearrange("p (b d) -> p b d", b=4)
                                last = mm(ps[e * 64:e * 64 + cap, 4 + dh, :], hidT[:, b, e * cap:(e + 1) * cap],
                                          w[:, b, dh * 512:(dh + 1) * 512], start=(b == 0), stop=(b == 3))
                    last.then_inc(p.down_done, 1)

                def spread(q, last_=False):
                    pe.wait_ge(p.giveT_ready, q + 1)
                    pe.wait_ge(p.y_ready, q + 1)
                    for s in range(4):
                        if s >= 2:
                            pe.wait_ge(p.added, 4 * q + s - 1)
                        for k in range(2):
                            bank = (2 if s % 2 else 4) + k
                            d = (2 * s + k) * P
                            last = mm(ps[:, bank, c0:L], ysb[:, d:d + P], giveT[:, c0:L], start=True, stop=True)
                        last.then_inc(p.spread, 1)
                        if last_ and s >= 2:
                            pe.wait_ge(p.added, 4 * q + s - 1)
                            for k in range(2 * s - 4, 2 * s - 2):
                                add_mean(2 * l + 1, k)
                    if last_:
                        for k in range(4, KD - 1):
                            if k % 2 == 0:
                                pe.wait_ge(p.added, 4 * q + k // 2 + 1)
                            add_mean(2 * l + 1, k)

                def finish_up(q, first):
                    if not first:
                        pe.wait_ge(p.added, 4 * q)
                    turn_hidden(q, 1)
                    turn_gates(q)

                def pair(i, q, first, second=False, last_=False):
                    pe.wait_ge(p.xg_ready, q + 1)
                    if first:
                        up(0, 7 * done + 1, 0)
                    else:
                        up(2, q, 0)
                        finish_up(q - 1, second)
                    if not last_:
                        gather(i + 1)
                    if second:
                        down(q - 1, None, done + 1)
                    elif not first:
                        down(q - 1, 0, 7 * done + i)
                    turn_hidden(q, 0)
                    up(1, q + 1, 1)
                    if not first:
                        pe.wait_ge(p.hidT_ready, 2 * q + 1)
                        spread(q - 1)

                q0 = done * PAIRS
                gather(0)
                pair(0, q0, True)
                pair(1, q0 + 1, False, second=True)
                with pe.Fori(2, PAIRS - 1) as i:
                    pair(i, q0 + i, False)
                qe = q0 + PAIRS - 1
                pair(PAIRS - 1, qe, False, last_=True)
                finish_up(qe, False)
                down(qe, 2, qe + 1)
                spread(qe, last_=True)
                pe.wait_ge(p.added, 4 * qe + 4)

            def moe(l, rounds_before):
                router(l)
                pe.wait_ge(s_htok, htok_before[l] + 2 * len(tiles_of(l)))
                moe_round(first_path, l, l)
                pe.wait_ge(s_routed, l + 1)
                further = pe.value_load(extra[0:1, 0:1], min_val=0, max_val=MAX_ROUNDS - 1)
                with pe.If(further > 0):
                    with pe.Fori(0, further) as rr:
                        moe_round(further_path, l, pe.snap(rounds_before + rr))
                return further

            if stop == "mamba":
                return
            further = moe(0, 0)
            layer_norm(1)
            if stop == "moe0":
                return
            for j in range(2 * KD):
                w = unit(BASE_A, j // 4).rearrange("p (k f) -> p k f", k=KD)
                if j % 4 == 0:
                    pe.wait_ge(R_A.full[(BASE_A + j // 4) % RING], fills(0, j // 4))
                if j >= 4:
                    pe.wait_ge(a["kq_e"], j - 3)
                c0 = 0 if j < KD else META
                if j >= SPLIT_FROM:
                    pe.wait_ge(a["wlo"], j - SPLIT_FROM + 1)
                    if j == SPLIT_FROM:
                        pe.wait_ge(a["hlo"], 2)
                for k in range(KD):
                    if j == 0:
                        pe.wait_ge(s_ln, KD + k + 1)
                    w_k = w[:, k, (j % 4) * P:(j % 4 + 1) * P]
                    if j < SPLIT_FROM:
                        last = mm(ps[:, j % 4, c0:L], w_k, hT[:, k, c0:L], start=(k == 0), stop=(k == KD - 1))
                        continue
                    w_hi, w_lo = w_high[:, j % 3, k, :], w_low[:, j % 2, k, :]
                    h_hi, h_lo = h_high[:, k, c0:L], h_low[:, k, c0:L]
                    mm(ps[:, j % 4, c0:L], w_hi, h_lo, start=(k == 0), stop=False)
                    mm(ps[:, j % 4, c0:L], w_lo, h_hi, start=False, stop=False)
                    last = mm(ps[:, j % 4, c0:L], w_hi, h_hi, start=False, stop=(k == KD - 1))
                last.then_inc(a["kq"], 1)
            def scores(j):
                b = 3 * (j % 2)
                if j >= 2:
                    pe.wait_ge(a["w"], j - 1)
                for h in range(2):
                    r_ = slice(64 * h, 64 * h + 64)
                    mm(ps[:, b + h, 0:256], kT[r_, j, META:META + P], qT[r_, j, :],
                       start=True, stop=False, skip_group_check=True)
                for h in range(2):
                    r_ = slice(64 * h, 64 * h + 64)
                    mm(ps[:, b + h, 256:384], kT[r_, j, META + P:L], qT[r_, j, P:SEQ],
                       start=False, stop=False, skip_group_check=True)
                mm(ps[0:64, b + 2, 0:256], kz[:, j, :], qT[:, j, :],
                   start=True, stop=False, skip_group_check=True).then_inc(a["z"], 1)

            for half in range(2):
                w = unit(BASE_A, 4 + half).rearrange("p (k f) -> p k f", k=KD)
                pe.wait_ge(R_A.full[(BASE_A + 4 + half) % RING], fills(0, 4 + half))
                for t, (o, n) in enumerate(TILES[1:]):
                    for k in range(KD):
                        last = mm(ps[:, 4 + 2 * half + t, :], hT[:, k, o:o + n], w[:, k, :],
                                  start=(k == 0), stop=(k == KD - 1))
                    last.then_inc(a["v"], 1)
                pe.wait_ge(a["kq_e"], 2 * KD)
                if half == 1:
                    pe.wait_ge(a["vz"], 2)
                for k in range(KD):
                    wk = w[:, k, :].rearrange("p (j h d) -> p j h d", j=4, h=2)
                    for h in range(2):
                        last = mm(ps[32 * h:32 * h + META, 3, 0:256], hT[:, k, 0:META], wk[:, :, h, :],
                                  start=(k == 0), stop=(k == KD - 1))
                last.then_inc(a["v0"], 1)
                if half == 0:
                    scores(0)
            pe.wait_ge(a["v_e"], 4)
            pe.wait_ge(a["vz"], 4)

            def log_weights(j):
                b, s_ = 3 * (j % 2), soft[:, j % 2, :]
                pe.wait_ge(a["sp"], j + 1)
                acc = dict(start=False, stop=False, skip_group_check=True)
                mm(ps[0:64, b + 2, 0:256], negfrom0[:, :], s_[0:64, 768:1024], **acc)
                for h in range(2):
                    s1, s2 = s_[:, 384 * h:384 * h + 256], s_[:, 384 * h + 256:384 * h + 384]
                    mm(ps[:, b + h, 0:256], negfrom[:, :], s1, **acc)
                    mm(ps[:, b + h, 128:256], negones[:, :], s2, **acc)
                    mm(ps[:, b + h, 256:384], negfrom[:, :], s2, **acc)
                    mm(ps[:, b + h, 0:128], ident[:, :], never[:, :], **acc)
                    mm(ps[:, b + h, 256:384], ident[:, :], never[:, :], **acc)
                    mm(ps[32 * h:32 * h + META, b + 2, 0:256], negones[:, 0:META], s1, **acc)
                    last = mm(ps[32 * h:32 * h + META, b + 2, 128:256], negones[:, 0:META], s2,
                              start=False, stop=True, skip_group_check=True)
                last.then_inc(a["arg"], 1)

            def values(j):
                w_ = wts[:, j % 2, :]
                o_ = ps[:, 6 + j % 2, :]
                pe.wait_ge(a["w"], j + 1)
                if j >= 2:
                    pe.wait_ge(a["o_e"], j - 1)
                mm(o_[:, 0:256], vz[:, j, :], w_[0:64, 768:1024], start=True, stop=False, skip_group_check=True)
                for h in range(2):
                    r_ = slice(64 * h, 64 * h + 64)
                    f = slice(j * P + 64 * h, j * P + 64 * h + 64)
                    mm(o_[r_, 0:256], vtok[:, 1, f], w_[:, 384 * h:384 * h + 256],
                       start=False, stop=False, skip_group_check=True)
                    last = mm(o_[r_, 128:256], vtok[:, 2, f], w_[:, 384 * h + 256:384 * h + 384],
                              start=False, stop=True, skip_group_check=True)
                last.then_inc(a["o"], 1)

            for j in range(KD):
                if j + 1 < KD:
                    scores(j + 1)
                log_weights(j)
                if j >= 1:
                    values(j - 1)
            values(KD - 1)
            pe.wait_ge(a["o_e"], KD)
            for mt in range(KD):
                w = unit(BASE_A, 6 + mt // 4).rearrange("p (k f) -> p k f", k=KD)
                if mt % 4 == 0:
                    pe.wait_ge(R_A.full[(BASE_A + 6 + mt // 4) % RING], fills(0, 6 + mt // 4))
                if mt >= 4:
                    pe.wait_ge(s_lnx, KD + mt - 3)
                for k in range(KD):
                    last = mm(ps[:, 4 + mt % 4, META:L], w[:, k, (mt % 4) * P:(mt % 4 + 1) * P], oT[:, k, :],
                              start=(k == 0), stop=(k == KD - 1))
                last.then_inc(a["outp"], 1)
                if mt > 0:
                    add_mean(2, mt - 1)
            layer_norm(2)
            if stop == "attn":
                return
            moe(1, further)
            layer_norm(3)
            n_ = 0
            for half in range(2):
                for t in (1, 2):
                    o, n = TILES[t]
                    for k in range(4):
                        pe.wait_ge(s_ln, 3 * KD + 4 * half + k + 1)
                        last = tr(ps[:, 2 + n_, k * P:(k + 1) * P], hT[:, 4 * half + k, o:o + n], ident[:, :])
                    last.then_inc(a["fin"], 1)
                    n_ += 1

        @block.scalar
        def _(act):
            sc = nc.scalar
            A = sc.activation
            link = Link(act, s_act)
            act.dma_start(prow[0:96, 0, :], mamba_conv_w[0].rearrange("w (c p) -> (w c) p", p=P)).then_inc(s_par, 16)
            act.dma_start(prow[96:120, 0, :], mamba_conv_b[0].rearrange("(c p) -> c p", p=P)).then_inc(s_par, 16)
            act.dma_start(dtb[:], mamba_dt_bias[0].rearrange("(e o) -> e o", o=1)).then_inc(s_ready0, 16)
            act.dma_start(alog[:], mamba_a_log[0].rearrange("(e o) -> e o", o=1)).then_inc(s_ready0, 16)
            for g6 in range(6):
                t, half = divmod(g6, 2)
                o, n = TILES[t]
                act.wait_ge(m["tin"], g6 + 1)
                A(hT[:, 4 * half:4 * half + 4, o:o + n],
                  ps[:, g6 % 4, :].rearrange("p (k n) -> p k n", k=4)[:, :, 0:n], ACT.Copy).then_inc(m["tin_e"], 1)
            act.wait_ge(s_ready0, 32)
            A(dtv[9][:, 0:1], alog[:, :], ACT.Exp).then_inc(m["dtea"], 1)
            act.wait_ge(m["dtn"], 1)
            A(dtv[2], dtv[1], ACT.Exp).then_inc(m["dtea"], 1)
            for c in range(CONV_TILES):
                if c == 13:
                    act.wait_ge(m["acp"], 1)
                    A(acT[:, :], ps[0:HEADS, 7, 0:L], ACT.Copy).then_inc(m["acs"], 1)
                    for t, (o, n) in enumerate(TILES):
                        A(dte[0:n, t, :], ps[0:n, 6, t * 32:t * 32 + 32], ACT.Exp).then_inc(m["dte_x"], 1)
                if c == 16:
                    for t in range(2):
                        n = TILES[t][1]
                        act.wait_ge(m["bt"], t + 1)
                        A(btok[0:n, t, :], ps[0:n, 4 + t, :], ACT.Copy).then_inc(m["btok"], 1)
                act.wait_ge(m["conv_done"], c + 1)
                dst = bcT[:, c, :] if c < 8 else xsT[:, c - 8, :]
                A(dst, convw[:, c % 3, :], ACT.Silu).then_inc(m["xbc"], 1)
            zt = 0

            def z_tile():
                nonlocal zt
                if zt < KI:
                    act.wait_ge(m["proj"], 1 + CONV_TILES + zt + 1)
                    if zt == 0:
                        act.wait_ge(m["da_r"], 3)
                    A(zT[:, zt, :], ps[:, 6 + zt % 2, 0:L], ACT.Copy).then_inc(m["z_read"], 1)
                    zt += 1

            z_tile()
            for q in range(3 * GROUPS):
                t, grp = divmod(q, GROUPS)
                n = TILES[t][1]
                if t >= 1:
                    act.wait_ge(m["bc"], q + 1)
                    if q > GROUPS:
                        act.wait_ge(m["yps"], q)
                    A(cdec[:, 0:4, 0:n], ps[:, 2, :].rearrange("p (h l) -> p h l", h=4)[:, :, 0:n], ACT.Exp)
                    A(cdec[:, 4:8, 0:n], ps[:, 3, :].rearrange("p (h l) -> p h l", h=4)[:, :, 0:n], ACT.Exp)\
                        .then_inc(m["expc"], 1)
                act.wait_ge(m["dd"], q + 1)
                d = decay[0:n, q % 2, :, 0:n]
                A(d, d, ACT.Exp).then_inc(m["expd"], 1)
                z_tile()
                if q < 3:
                    z_tile()
            act.wait_ge(m["z_read"], KI)
            for grp in range(GROUPS):
                zg = zT[:, 4 * grp:4 * grp + 4, :]
                A(zg, zg, ACT.Silu).then_inc(m["zsilu"], 1)
            for grp in range(GROUPS):
                act.wait_ge(m["yz"], grp + 1)
                A(squares(grp), zT[:, 4 * grp:4 * grp + 4, :], ACT.Square).then_inc(m["rsq"], 1)
            sc.preload_act_table(ACT.Sqrt)
            for grp in range(GROUPS):
                act.wait_ge(m["rps"], grp + 1)
                A(rms(grp, 0), ps[:, grp, 0:L], ACT.Sqrt, bias=epsc[:, 0:1]).then_inc(m["rsd"], 1)
            for grp in range(GROUPS):
                act.wait_ge(m["yn"], 4 * grp + 4)
                A(y_high[:, 4 * grp:4 * grp + 4, :], zT[:, 4 * grp:4 * grp + 4, :], ACT.Copy).then_inc(m["yhi"], 1)
            for u in range(2 * (KD - OUT_FROM)):
                n_unit, w = out_weights(u)
                act.wait_ge(R_M.full[n_unit % RING], fills(BASE_M, n_unit))
                if u >= 2:
                    if u % 2 == 0:
                        act.wait_ge(m["half"], u // 2)
                    else:
                        act.wait_ge(m["outp"], OUT_FROM + u // 2)
                A(wo_high[:, u % 2, :, :], w, ACT.Copy).then_inc(m["whi"], 1)

            def layer_norm(i):
                c0 = C0[i // 2]
                col = 16 + (i % 2) * 32 + (i // 2) * 8
                sc.preload_act_table(ACT.Sqrt)
                for quarter in range(4):
                    act.wait_ge(s_lnc, 4 * i + quarter + 1)
                    ks = slice(2 * quarter, 2 * quarter + 2)
                    A(sq[:, ks, c0:L], rT[:, ks, c0:L], ACT.Square).then_inc(s_lnq, 1)
                act.wait_ge(s_lnv, i + 1)
                A(stat[:, 0, c0:L], ps[:, 1, c0:L], ACT.Sqrt, bias=epsc[:, 0:1]).then_inc(s_lns, 1)
                for k in range(KD):
                    act.wait_ge(s_lnn, KD * i + k + 1)
                    A(hT[:, k, c0:L], rT[:, k, c0:L], ACT.Identity, scale=par2[:, col + k:col + k + 1],
                      bias=par2[:, col + 16 + k:col + 17 + k]).then_inc(s_ln, 1)

            layer_norm(0)

            def router(l):
                c0 = C0[l]
                act.wait_ge(s_router, l + 1)
                if l == 0:
                    act.wait_ge(s_rw, 32)
                A(logit[:, c0:L], ps[0:N_EXP, 2, c0:L], ACT.Identity, bias=rbias[:, 0:1]).then_inc(s_logit, 1)
                sc.preload_act_table(ACT.Exp)
                act.wait_ge(s_below, l + 1)
                A(route[:, 1, :], route[:, 1, :], ACT.Exp).then_inc(s_numer, 1)
                g_ = 0
                for t, o, n in tiles_of(l):
                    for half in range(2):
                        act.wait_ge(s_htok_ps, htok_before[l] + g_ + 1)
                        A(tok[0:n, t, 512 * half:512 * half + 512], ps[0:n, 4 + g_ % 2, :], ACT.Copy)\
                            .then_inc(s_htok, 1)
                        g_ += 1

            def moe_round(p, l, done):
                c0 = C0[l]

                def take_xg(q):
                    act.wait_ge(p.gathered, q + 1)
                    A(xg[:, 0:4, :], ps[:, 6, :].rearrange("p (k c) -> p k c", k=4)[:, :, 0:2 * cap], ACT.Copy)
                    A(xg[:, 4:8, :], ps[:, 7, :].rearrange("p (k c) -> p k c", k=4)[:, :, 0:2 * cap], ACT.Copy)\
                        .then_inc(p.xg_ready, 1)

                def silu(q, half):
                    act.wait_ge(p.up_done, 2 * q + half + 1)
                    A(sg[:, half, :], ps[:, half, 0:HALF], ACT.Silu).then_inc(p.silu_done, 1)

                def take_hidT(q, half):
                    act.wait_ge(p.hid_turned, 2 * q + half + 1)
                    A(hidT[:, 2 * half:2 * half + 2, :], ps[:, 2, 0:256].rearrange("p (a b) -> p a b", a=2), ACT.Copy)\
                        .then_inc(p.hidT_ready, 1)

                def finish(q):
                    take_hidT(q, 1)
                    act.wait_ge(p.give_turned, q + 1)
                    A(giveT[:, c0:L], ps[:, 3, c0:L], ACT.Copy).then_inc(p.giveT_ready, 1)
                    act.wait_ge(p.down_done, q + 1)
                    A(ysb.rearrange("p (a b) -> p a b", a=2), ps[:, 4:6, :], ACT.Copy).then_inc(p.y_ready, 1)

                def pair(q, first, last_):
                    silu(q, 0)
                    if not first:
                        finish(q - 1)
                    take_hidT(q, 0)
                    silu(q, 1)
                    if not last_:
                        take_xg(q + 1)

                q0 = done * PAIRS
                take_xg(q0)
                pair(q0, True, False)
                with act.Fori(1, PAIRS - 1) as i:
                    pair(q0 + i, False, False)
                qe = q0 + PAIRS - 1
                pair(qe, False, True)
                finish(qe)

            def moe(l, rounds_before):
                router(l)
                moe_round(first_path, l, l)
                act.wait_ge(s_routed, l + 1)
                further = act.value_load(extra[0:1, 0:1], min_val=0, max_val=MAX_ROUNDS - 1)
                with act.If(further > 0):
                    with act.Fori(0, further) as rr:
                        moe_round(further_path, l, act.snap(rounds_before + rr))
                return further

            if stop == "mamba":
                return
            further = moe(0, 0)
            layer_norm(1)
            if stop == "moe0":
                return
            for half in range(2):
                ks = slice(4 * half, 4 * half + 4)
                act.wait_ge(s_ln, KD + 4 * half + 4)
                A(h_high[:, ks, :], hT[:, ks, :], ACT.Copy).then_inc(a["hhi"], 1)
            for j in range(SPLIT_FROM, 2 * KD):
                act.wait_ge(R_A.full[(BASE_A + j // 4) % RING], fills(0, j // 4))
                if j >= SPLIT_FROM + 3:
                    act.wait_ge(a["kq"], j - 2)
                w = unit(BASE_A, j // 4).rearrange("p (k f) -> p k f", k=KD)
                A(w_high[:, j % 3, :, :], w[:, :, (j % 4) * P:(j % 4 + 1) * P], ACT.Copy)\
                    .then_inc(a["whi"], 1)

            def soft_log(j):
                act.wait_ge(a["bound"], j + 1)
                parts = (soft[:, j % 2, 0:768], soft[0:64, j % 2, 768:1024])
                for v in parts:
                    A(v, v, ACT.Exp).then_inc(a["e"], 1)
                act.wait_ge(a["e"], 2 * j + 2)
                A(parts[0], parts[0], ACT.Ln, bias=1.0)
                A(parts[1], parts[1], ACT.Ln, bias=1.0).then_inc(a["ln"], 1)

            def weights(j):
                b = 3 * (j % 2)
                act.wait_ge(a["arg"], j + 1)
                if j >= 2:
                    act.wait_ge(a["o"], j - 1)
                A(wts[:, j % 2, 0:768].rearrange("p (h q) -> p h q", h=2), ps[:, b:b + 2, 0:384], ACT.Exp)
                A(wts[0:64, j % 2, 768:1024], ps[0:64, b + 2, 0:256], ACT.Exp).then_inc(a["w"], 1)

            act.wait_ge(a["blocks"], 1)
            sc.preload_act_table_set("natural_log_exp_and_others")
            for half in range(2):
                for t in (1, 2):
                    act.wait_ge(a["v"], 2 * half + t)
                    A(vtok[:, t, 512 * half:512 * half + 512], ps[:, 3 + 2 * half + t, :], ACT.Copy).then_inc(a["v_e"], 1)
                act.wait_ge(a["v0"], half + 1)
                for h in range(2):
                    A(vz[32 * h:32 * h + META, 4 * half:4 * half + 4, 64 * h:64 * h + 64],
                      ps[32 * h:32 * h + META, 3, 0:256].rearrange("p (j d) -> p j d", j=4), ACT.Copy)\
                        .then_inc(a["vz"], 1)
                if half == 0:
                    soft_log(0)
            for j in range(KD):
                if j + 1 < KD:
                    soft_log(j + 1)
                weights(j)
            layer_norm(2)
            if stop == "attn":
                return
            moe(1, further)
            layer_norm(3)
            for n_ in range(4):
                half, t = n_ // 2, 1 + n_ % 2
                act.wait_ge(a["fin"], n_ + 1)
                A(tok[:, t, 512 * half:512 * half + 512], ps[:, 2 + n_, :], ACT.Copy).then_inc(a["fin_e"], 1)
                act.wait_ge(a["fin_e"], n_ + 1)
                act.dma_start(out[0, (t - 1) * P:t * P, 512 * half:512 * half + 512],
                              tok[:, t, 512 * half:512 * half + 512]).then_inc(a["store"], 16)
            act.wait_ge(a["store"], 64)

        @block.vector
        def _(dve):
            v = nc.vector
            link = Link(dve, s_dve)
            tt, ts, stt = v.tensor_tensor, v.tensor_scalar, v.scalar_tensor_tensor
            dve.wait_ge(m["ptr"], 1)
            v.tensor_copy(par1[:, :], ps[:, 4, 0:120]).then_inc(m["ptr_e"], 1)
            dve.wait_ge(m["ptr_e"], 1)
            dve.wait_ge(s_ready0, 32)
            dve.wait_ge(m["proj"], 1)
            ts(dtv[0], ps[0:HEADS, 0, 0:L], dtb[:, 0:1], None, ALU.add).then_inc(m["dtx"], 1)
            dve.wait_ge(m["dtx"], 1)
            stt(dtv[1], dtv[0], -1.0, dtv[0], ALU.mult, ALU.min).then_inc(m["dtn"], 1)

            def conv(c):
                ct = KI + c if c < 8 else c - 8
                src, dst = ps[:, 1 + c % 3, :], convw[:, c % 3, :]
                dve.wait_ge(m["proj"], c + 2)
                if c >= 3:
                    dve.wait_ge(m["xbc"], c - 2)
                tap = [par1[:, 24 * w + ct:24 * w + ct + 1] for w in range(CONV_W)]
                link(ts(dst, src[:, 0:L], tap[3], par1[:, 96 + ct:97 + ct], ALU.mult, ALU.add))
                for back in (1, 2, 3):
                    ins = stt(dst[:, back:L], src[:, 0:L - back], tap[3 - back], dst[:, back:L], ALU.mult, ALU.add)
                    if back < 3:
                        link(ins)
                    else:
                        ins.then_inc(m["conv_done"], 1)

            def dt_chain(part):
                x_, _, e_, d_, r_, s_, s2, p_, q_, ea = dtv
                if part == 0:
                    dve.wait_ge(m["dtea"], 2)
                    link(ts(d_, e_, 2.0, None, ALU.add))
                    link(v.reciprocal(r_, d_))
                if part == 1:
                    link(tt(s_, e_, r_, ALU.mult))
                    link(tt(s2, s_, s_, ALU.mult))
                    link(ts(p_, s2, 1.0 / 15, None, ALU.mult))
                if part in (2, 3):
                    for c_ in ((13, 11, 9), (7, 5, 3))[part - 2]:
                        link(stt(p_, p_, 1.0 / c_, s2, ALU.add, ALU.mult))
                if part == 4:
                    link(stt(q_, p_, 1.0, s_, ALU.add, ALU.mult))
                    link(ts(q_, q_, 2.0, None, ALU.mult))
                    link(stt(daT[0:HEADS], x_, 0.0, q_, ALU.max, ALU.add))
                    ts(daT[HEADS:2 * HEADS], daT[0:HEADS], ea[:, 0:1], -1.0, ALU.mult, ALU.mult)\
                        .then_inc(m["daT_r"], 1)

            for c in range(CONV_TILES):
                conv(c)
                if 1 <= c < 6:
                    dt_chain(c - 1)
                if c == 4:
                    dve.wait_ge(m["ptr"], 2)
                    v.tensor_copy(par2[:, :], ps[:, 4, 128:208]).then_inc(m["ptr_e"], 1)
                    dve.wait_ge(m["ptr_e"], 2)
                if c == 8:
                    dve.wait_ge(m["da_t"], 1)
                    for t, (o, n) in enumerate(TILES):
                        v.tensor_copy(da[0:n, t, :], ps[0:n, 5, t * 64:t * 64 + 64]).then_inc(m["da_r"], 1)
                if c == 11:
                    dve.wait_ge(m["acp"], 1)
                    for t, (o, n) in enumerate(TILES):
                        v.tensor_copy(acum[0:n, t, :], ps[0:n, 6, 96 + t * 32:128 + t * 32]).then_inc(m["acr"], 1)
            dve.wait_ge(m["acr"], 3)
            dve.wait_ge(m["xbc"], CONV_TILES)
            dve.wait_ge(s_skip, 32)

            def ssd_back(q):
                t, grp = divmod(q, GROUPS)
                o, n = TILES[t]
                dve.wait_ge(m["yps"], q + 1)
                for k in range(4):
                    j = grp * 4 + k
                    ins = stt(xsT[:, j, o:o + n], xsT[:, j, o:o + n], dskip[:, j:j + 1],
                              ps[:, 4, k * P:k * P + n], ALU.mult, ALU.add)
                ins.then_inc(m["yadd"], 1)
                if t < 2:
                    dve.wait_ge(m["stps"], q + 1)
                    if t == 0:
                        v.tensor_copy(state[:, grp * HPG:(grp + 1) * HPG, :],
                                      ps[:, 5, :].rearrange("p (h d) -> p h d", h=HPG)).then_inc(m["stup"], 1)
                    else:
                        dve.wait_ge(m["stup"], q)
                        for h in range(HPG):
                            s_ = state[:, grp * HPG + h, :]
                            ins = stt(s_, s_, lastd[:, q % 2, h:h + 1], ps[:, 5, h * HD:(h + 1) * HD],
                                      ALU.mult, ALU.add)
                        ins.then_inc(m["stup"], 1)

            for q in range(3 * GROUPS):
                t, grp = divmod(q, GROUPS)
                o, n = TILES[t]
                hs = slice(grp * HPG, (grp + 1) * HPG)
                dve.wait_ge(m["xtr"], q + 1)
                if q >= GROUPS:
                    dve.wait_ge(m["yps"], q - GROUPS + 1)
                    dve.wait_ge(m["xde"], q - GROUPS + 1)
                tt(xdt[0:n, hs, :], ps[0:n, 0, :].rearrange("p (h d) -> p h d", h=HPG),
                   da[0:n, t, hs].unsqueeze(2).broadcast_to([n, HPG, HD]), ALU.mult).then_inc(m["xdt"], 1)
                dve.wait_ge(m["cb"], q + 1)
                if q > 0:
                    dve.wait_ge(m["mt"], q)
                tt(cbm[0:n, 0:n], ps[0:n, 1, 0:n], upto[0:n, 0:n], ALU.mult).then_inc(m["cbm"], 1)
                dve.wait_ge(m["bc"], q + 1)
                if q >= 2:
                    dve.wait_ge(m["yps"], q - 1)
                if t >= 1:
                    dve.wait_ge(m["expc"], q - GROUPS + 1)
                for h in range(HPG):
                    hh = grp * HPG + h
                    ins = ts(decay[0:n, q % 2, h, 0:n], ps[0:n, 2 + h // 4, (h % 4) * P:(h % 4) * P + n],
                             acum[0:n, t, hh:hh + 1], 0.0, ALU.subtract, ALU.min)
                ins.then_inc(m["dd"], 1)
                if t >= 1:
                    if t == 1:
                        dve.wait_ge(m["stup"], q - 1)
                        link(v.tensor_copy(lastd[:, q % 2, :], cdec[:, :, n - 1]))
                    tt(cdec[:, :, 0:n], cdec[:, :, 0:n],
                       bcT[:, GROUPS + grp, o:o + n].unsqueeze(1).broadcast_to([P, HPG, n]),
                       ALU.mult).then_inc(m["cs"], 1)
                if q > 0:
                    ssd_back(q - 1)
            for grp in range(GROUPS):
                if grp == GROUPS - 1:
                    ssd_back(3 * GROUPS - 1)
                dve.wait_ge(m["yadd"], 2 * GROUPS + grp + 1)
                dve.wait_ge(m["zsilu"], grp + 1)
                g4 = slice(4 * grp, 4 * grp + 4)
                tt(zT[:, g4, :], zT[:, g4, :], xsT[:, g4, :], ALU.mult).then_inc(m["yz"], 1)
            for grp in range(GROUPS):
                dve.wait_ge(m["rsd"], grp + 1)
                link(v.reciprocal(rms(grp, 1), rms(grp, 0)))
                for k in range(4):
                    j = 4 * grp + k
                    stt(zT[:, j, :], zT[:, j, :], par2[:, j:j + 1], rms(grp, 1), ALU.mult, ALU.mult)\
                        .then_inc(m["yn"], 1)

            dve.wait_ge(m["yn"], KI)
            for grp in range(GROUPS):
                dve.wait_ge(m["yhi"], grp + 1)
                g4 = slice(4 * grp, 4 * grp + 4)
                tt(y_low[:, g4, :], zT[:, g4, :], y_high[:, g4, :].bitcast(F32), ALU.subtract).then_inc(m["ylo"], 1)

            def low_out_weights(u):
                dve.wait_ge(m["whi"], u + 1)
                w = out_weights(u)[1]
                for part in range(2):
                    ks = slice(4 * part, 4 * part + 4)
                    ins = tt(wo_low[u % 2][part], w[:, ks, :], wo_high[:, u % 2, ks, :].bitcast(F32), ALU.subtract)
                ins.then_inc(m["wlo"], 1)

            def residual(i, done):
                c0 = C0[i // 2]
                for mt in range(KD):
                    if i == 0 and (mt == 0 or OUT_FROM <= mt < KD - 1):
                        nxt = OUT_FROM if mt == 0 else mt + 1
                        for half in range(2):
                            low_out_weights(2 * (nxt - OUT_FROM) + half)
                    dve.wait_ge(done, mt + 1)
                    stt(rT[:, mt, c0:L], hT[:, mt, c0:L], ALPHA, ps[:, 4 + mt % 4, c0:L], ALU.mult, ALU.add)\
                        .then_inc(s_lnx, 1)

            def layer_norm(i):
                c0 = C0[i // 2]
                n = L - c0
                dve.wait_ge(s_lnm, i + 1)
                for quarter in range(4):
                    ks = slice(2 * quarter, 2 * quarter + 2)
                    tt(rT[:, ks, c0:L], rT[:, ks, c0:L], ps[:, 0, c0:L].unsqueeze(1).broadcast_to([P, 2, n]),
                       ALU.subtract).then_inc(s_lnc, 1)
                dve.wait_ge(s_lnc, 4 * i + 4)
                dve.wait_ge(s_lns, i + 1)
                link(v.reciprocal(stat[:, 1, c0:L], stat[:, 0, c0:L]))
                for k in range(KD):
                    tt(rT[:, k, c0:L], rT[:, k, c0:L], stat[:, 1, c0:L], ALU.mult).then_inc(s_lnn, 1)
                dve.wait_ge(s_ln, KD * (i + 1))

            residual(0, m["outp"])
            layer_norm(0)

            def place(x_, groups, out_, higher_first, buf):
                pi = x_.unsqueeze(2).broadcast_to([P, groups, 4, 4])
                pj = x_.unsqueeze(3).broadcast_to([P, groups, 4, 4])
                c0_, c1_ = (cmpb[:, n, 0:16 * groups].rearrange("p (g j i) -> p g j i", g=groups, j=4) for n in (0, 1))
                link(tt(c0_, pi, pj, ALU.is_gt))
                link(tt(c1_, pi, pj, ALU.is_ge))
                link(tt(c0_, c0_, higher[:, :, :].unsqueeze(1).broadcast_to([P, groups, 4, 4]), ALU.mult))
                link(tt(c1_, c1_, lower[:, :, :].unsqueeze(1).broadcast_to([P, groups, 4, 4]), ALU.mult))
                link(tt(c0_, c0_, c1_, ALU.add))
                link(v.tensor_reduce(out_, c0_, AX.X, ALU.add))

            def router(l):
                c0 = C0[l]
                link(v.memset(route[:, :, :], 0.0))
                link(v.memset(rank[:, :, :], -1.0))
                link(v.memset(gate[:, :, :], 0.0))
                link(ts(rT[:, :, c0:L], hT[:, :, c0:L], ALPHA, None, ALU.mult))
                t3 = [route[:, n, :].rearrange("p (t e) -> p t e", t=3) for n in range(12)]
                g12 = [route[:, n, :].rearrange("p (g j) -> p g j", j=PER_GRP) for n in range(12)]
                dve.wait_ge(s_turned, l + 1)
                parts = [(META, slice(0, 1))][l:] + [(P, slice(1, 3))]
                ps3 = ps[:, 3, 0:3 * N_EXP].rearrange("p (t e) -> p t e", t=3)
                ps2 = ps[:, 2, 0:3 * N_EXP].rearrange("p (t e) -> p t e", t=3)
                for n, t in parts:
                    link(v.tensor_copy(t3[0][0:n, t, :], ps3[0:n, t, :]))
                top = route[:, 9, 0:3]
                link(v.tensor_reduce(top, t3[0], AX.X, ALU.max))
                tt(t3[1], t3[0], top.unsqueeze(2).broadcast_to([P, 3, N_EXP]), ALU.subtract).then_inc(s_below, 1)
                dve.wait_ge(s_numer, l + 1)
                total, inv = route[:, 9, 3:6], route[:, 9, 6:9]
                link(v.tensor_reduce(total, t3[1], AX.X, ALU.add))
                link(v.reciprocal(inv, total))
                link(tt(t3[2], t3[1], inv.unsqueeze(2).broadcast_to([P, 3, N_EXP]), ALU.mult))
                place(g12[2], 12, g12[3], None, 0)
                link(ts(t3[3], t3[3], 2.0, None, ALU.is_lt))
                link(tt(t3[4], t3[3], t3[2], ALU.mult))
                score, placed = route[:, 5, 0:12], route[:, 6, 0:12]
                link(v.tensor_reduce(score, g12[4], AX.X, ALU.add))
                place(score.rearrange("p (t g) -> p t g", t=3), 3, placed.rearrange("p (t g) -> p t g", t=3), None, 0)
                link(ts(placed, placed, 1.0, None, ALU.is_lt))
                tt(g12[8], g12[3], placed.unsqueeze(2).broadcast_to([P, 12, PER_GRP]), ALU.mult).then_inc(s_chosen, 1)
                dve.wait_ge(s_chosen, l + 1)
                link(tt(t3[7], t3[8], t3[2], ALU.mult))
                link(v.tensor_reduce(total, t3[7], AX.X, ALU.add))
                for n, t in parts:
                    w = t.stop - t.start
                    link(v.reciprocal(inv[0:n, t], total[0:n, t]))
                    link(tt(gate[0:n, t, 0:N_EXP], t3[7][0:n, t, :],
                            inv[0:n, t].unsqueeze(2).broadcast_to([n, w, N_EXP]), ALU.mult))
                dve.wait_ge(s_counted, l + 1)
                for n, t in parts:
                    link(stt(t3[10][0:n, t, :], ps2[0:n, t, :], 1.0, t3[8][0:n, t, :], ALU.add, ALU.mult))
                    link(ts(rank[0:n, t, 0:N_EXP], t3[10][0:n, t, :], -1.0, None, ALU.add))

            def count_rounds(l):
                link(v.tensor_reduce(rmax[0:1, 0:1], ps[0:1, 2, 3 * N_EXP:4 * N_EXP], AX.X, ALU.max))
                link(ts(rmax[0:1, 1:2], rmax[0:1, 0:1], float(step), None, ALU.is_gt))
                for k in range(2, MAX_ROUNDS):
                    link(stt(rmax[0:1, 1:2], rmax[0:1, 0:1], float(step * k), rmax[0:1, 1:2], ALU.is_gt, ALU.add))
                v.tensor_copy(extra[0:1, 0:1], rmax[0:1, 1:2]).then_inc(s_routed, 1)
                dve.wait_ge(s_routed, l + 1)

            def moe_round(p, l, done, again):
                tl = tiles_of(l)
                c0 = C0[l]

                def make_pick(i):
                    for t, o, n in tl:
                        for k in range(2):
                            ins = ts(pick[0:n, t, k * cap:(k + 1) * cap], slots[0:n, :],
                                     rank[0:n, t, bass.ds(2 * i + k, 1)], None, ALU.is_equal)
                    ins.then_inc(p.pick_ready, 1)

                def make_give(i):
                    for t, o, n in tl:
                        for k in range(2):
                            ins = ts(give[0:n, t, k * cap:(k + 1) * cap], slots[0:n, :],
                                     rank[0:n, t, bass.ds(2 * i + k, 1)], gate[0:n, t, bass.ds(2 * i + k, 1)],
                                     ALU.is_equal, ALU.mult)
                    ins.then_inc(p.give_ready, 1)

                def make_hidden(q, half):
                    dve.wait_ge(p.silu_done, 2 * q + half + 1)
                    tt(hid[:, half, :], sg[:, half, :], ps[:, half, HALF:2 * HALF], ALU.mult)\
                        .then_inc(p.hid_ready, 1)

                def add(q):
                    for s in range(4):
                        dve.wait_ge(p.spread, 4 * q + s + 1)
                        r_ = rT[:, 2 * s:2 * s + 2, c0:L]
                        b0 = 2 if s % 2 else 4
                        tt(r_, r_, ps[:, b0:b0 + 2, c0:L], ALU.add).then_inc(p.added, 1)

                def pair(i, q, first, last_):
                    make_hidden(q, 0)
                    if not first:
                        dve.wait_ge(p.give_turned, q)
                        make_give(i)
                    if not last_:
                        dve.wait_ge(p.gathered, q + 2)
                        make_pick(i + 2)
                    make_hidden(q, 1)
                    if not first:
                        add(q - 1)

                if again:
                    ts(rank[:, :, :], rank[:, :, :], -float(step), None, ALU.add).then_inc(s_ranked, 1)
                    dve.wait_ge(s_ranked, done + 1)
                q0 = done * PAIRS
                make_pick(0)
                if not again:
                    count_rounds(l)
                make_give(0)
                dve.wait_ge(p.gathered, q0 + 1)
                make_pick(1)
                pair(0, q0, True, False)
                with dve.Fori(1, PAIRS - 1) as i:
                    pair(i, q0 + i, False, False)
                qe = q0 + PAIRS - 1
                pair(PAIRS - 1, qe, False, True)
                add(qe)
                dve.wait_ge(p.added, 4 * qe + 4)

            def moe(l, rounds_before):
                router(l)
                moe_round(first_path, l, l, False)
                further = dve.value_load(extra[0:1, 0:1], min_val=0, max_val=MAX_ROUNDS - 1)
                with dve.If(further > 0):
                    with dve.Fori(0, further) as rr:
                        moe_round(further_path, l, dve.snap(rounds_before + rr), True)
                return further

            if stop == "mamba":
                return
            further = moe(0, 0)
            layer_norm(1)
            if stop == "moe0":
                return
            v.memset(kz, 0.0)
            v.memset(vz, 0.0).then_inc(a["blocks"], 1)
            dve.wait_ge(a["blocks"], 1)
            for half in range(2):
                ks = slice(4 * half, 4 * half + 4)
                dve.wait_ge(a["hhi"], half + 1)
                tt(h_low[:, ks, :], hT[:, ks, :], h_high[:, ks, :].bitcast(F32), ALU.subtract).then_inc(a["hlo"], 1)

            def low_weights(j):
                dve.wait_ge(a["whi"], j - SPLIT_FROM + 1)
                w = unit(BASE_A, j // 4).rearrange("p (k f) -> p k f", k=KD)[:, :, (j % 4) * P:(j % 4 + 1) * P]
                tt(w_low[:, j % 2, :, :], w, w_high[:, j % 3, :, :].bitcast(F32), ALU.subtract).then_inc(a["wlo"], 1)

            low_weights(SPLIT_FROM)
            for j in range(2 * KD):
                dve.wait_ge(a["kq"], j + 1)
                if j < KD:
                    for h in range(2):
                        r_ = slice(64 * h, 64 * h + 64)
                        v.tensor_copy(kz[r_, j, 32 * h:32 * h + META], ps[r_, j % 4, 0:META])
                    v.tensor_copy(kT[:, j, :], ps[:, j % 4, 0:L]).then_inc(a["kq_e"], 1)
                else:
                    ts(qT[:, j - KD, :], ps[:, j % 4, META:L], HD ** -0.5, None, ALU.mult).then_inc(a["kq_e"], 1)
                if SPLIT_FROM < j + 2 < 2 * KD:
                    low_weights(j + 2)

            def bound(j):
                b, s_ = 3 * (j % 2), soft[:, j % 2, :]
                dve.wait_ge(a["z"], j + 1)
                if j >= 2:
                    dve.wait_ge(a["arg"], j - 1)
                ts(s_[:, 0:768].rearrange("p (h q) -> p h q", h=2), ps[:, b:b + 2, 0:384], TOP, None, ALU.min)
                ts(s_[0:64, 768:1024], ps[0:64, b + 2, 0:256], TOP, None, ALU.min)\
                    .then_inc(a["bound"], 1)

            def softplus(j):
                b, s_ = 3 * (j % 2), soft[:, j % 2, :]
                dve.wait_ge(a["ln"], j + 1)
                s2 = s_[:, 0:768].rearrange("p (h q) -> p h q", h=2)
                tt(s2, ps[:, b:b + 2, 0:384], s2, ALU.max)
                link(tt(s_[0:64, 768:1024], ps[0:64, b + 2, 0:256], s_[0:64, 768:1024], ALU.max))
                mask = before[:, :].unsqueeze(1).broadcast_to([P, 2, P])
                tt(s2[:, :, 0:P], s2[:, :, 0:P], mask, ALU.mult)
                tt(s2[:, :, 256:384], s2[:, :, 256:384], mask, ALU.mult).then_inc(a["sp"], 1)

            def take_o(j):
                dve.wait_ge(a["o"], j + 1)
                v.tensor_copy(oT[:, j, :], ps[:, 6 + j % 2, 0:256]).then_inc(a["o_e"], 1)

            bound(0)
            for j in range(KD):
                softplus(j)
                if j + 1 < KD:
                    bound(j + 1)
                if j >= 1:
                    take_o(j - 1)
            take_o(KD - 1)
            residual(2, a["outp"])
            layer_norm(2)
            if stop == "attn":
                return
            moe(1, further)
            layer_norm(3)


_INS = ["x", "meta_tokens", "mamba_w_in", "mamba_conv_w", "mamba_conv_b", "mamba_dt_bias", "mamba_a_log",
        "mamba_d_skip", "mamba_norm_w", "mamba_w_out", "sb_w_q", "sb_w_o", "shared_w_k", "shared_w_v",
        "ln_mix_g", "ln_mix_b", "ln_ffn_g", "ln_ffn_b", "router_w", "router_b", "moe_w_gate", "moe_w_up",
        "moe_w_down"]


def kernel(**inputs):
    import numpy as _np
    import concourse.bacc as _bacc
    from concourse import mybir as _mybir
    from concourse.bass_utils import run_bass_kernel_spmd as _run

    nc = _bacc.Bacc("TRN2", target_bir_lowering=False, num_devices=1)
    arrays, args = {}, []
    for name in _INS:
        a = _np.ascontiguousarray(inputs[name])
        arrays[f"in_{name}_dram"] = a
        args.append(nc.dram_tensor(f"in_{name}_dram", a.shape, _mybir.dt.from_np(a.dtype), kind="ExternalInput").ap())
    args.append(nc.dram_tensor("out_dram", (1, SEQ, D_MODEL), _mybir.dt.float32, kind="ExternalOutput").ap())
    build_trunk(nc, *args)
    r = _run(nc, [arrays], core_ids=[0])
    return r.results[0]["out_dram"]
```
